# Optimizing a Trainium2 kernel written in Bass

```python
import math
import jax, jax.numpy as jnp
from jax import lax
import numpy as np

D_MODEL = 1024
BATCH = 1
SEQ = 512
DEPTH = 1

MEM_LEN = 256
HEAD_DIM = 64
ATTN_WIDTH = D_MODEL // 2
N_Q_HEADS = ATTN_WIDTH // HEAD_DIM
N_KV_HEADS = N_Q_HEADS // 4
Q_PER_KV = N_Q_HEADS // N_KV_HEADS
WINDOW = 128
BLOCK = 128
CONV_CH = D_MODEL // 4
CONV_WIDTH = 31
MEM_WIDTH = D_MODEL // 4
N_MEM_HEADS = MEM_WIDTH // HEAD_DIM
MIX_WIDTH = ATTN_WIDTH + CONV_CH + MEM_WIDTH
ROPE_THETA = 500000.0
ROPE_DIM = HEAD_DIM // 4
D_FF = 256 * math.ceil(8 * D_MODEL / 3 / 256)
EPS = 1e-6

Q_COLS = N_Q_HEADS * HEAD_DIM
KV_COLS = N_KV_HEADS * HEAD_DIM
GLU_COLS = 2 * CONV_CH
MQ_COLS = N_MEM_HEADS * HEAD_DIM
IN_COLS = Q_COLS + 2 * KV_COLS + GLU_COLS + MQ_COLS
SPLITS = [Q_COLS, Q_COLS + KV_COLS, Q_COLS + 2 * KV_COLS, Q_COLS + 2 * KV_COLS + GLU_COLS]


def rms_norm(x, g):
    xf = x.astype(jnp.float32)
    y = xf * lax.rsqrt(jnp.mean(xf * xf, axis=-1, keepdims=True) + EPS)
    return (y * g.astype(jnp.float32)).astype(x.dtype)

def layer_norm(x, g, b):
    xf = x.astype(jnp.float32)
    mu = jnp.mean(xf, axis=-1, keepdims=True)
    var = jnp.mean(jnp.square(xf - mu), axis=-1, keepdims=True)
    y = (xf - mu) * lax.rsqrt(var + EPS)
    return (y * g.astype(jnp.float32) + b.astype(jnp.float32)).astype(x.dtype)

def swiglu(x, w_gate, w_up, w_down):
    return (jax.nn.silu(x @ w_gate) * (x @ w_up)) @ w_down

def rope_partial(x, positions):
    half = ROPE_DIM // 2
    inv_freq = ROPE_THETA ** (-jnp.arange(half, dtype=jnp.float32) / half)
    ang = positions.astype(jnp.float32)[..., None] * inv_freq
    cos = jnp.cos(ang)[:, :, None, :]
    sin = jnp.sin(ang)[:, :, None, :]
    xr = x[..., :ROPE_DIM].astype(jnp.float32)
    x1, x2 = xr[..., :half], xr[..., half:]
    rot = jnp.concatenate([x1 * cos - x2 * sin, x2 * cos + x1 * sin], axis=-1).astype(x.dtype)
    return jnp.concatenate([rot, x[..., ROPE_DIM:]], axis=-1)

def sliding_window_attention(q, k, v, sinks):
    B, T = q.shape[0], q.shape[1]
    nb = T // BLOCK
    qb = q.reshape(B, nb, BLOCK, N_KV_HEADS, Q_PER_KV, HEAD_DIM)

    def with_prev(a):
        a = a.reshape(B, nb, BLOCK, N_KV_HEADS, HEAD_DIM)
        prev = jnp.pad(a, ((0, 0), (1, 0), (0, 0), (0, 0), (0, 0)))[:, :-1]
        return jnp.concatenate([prev, a], axis=2)

    kb, vb = with_prev(k), with_prev(v)
    s = jnp.einsum('bnqgrd,bnkgd->bngrqk', qb, kb).astype(jnp.float32) * (HEAD_DIM ** -0.5)
    qi = jnp.arange(BLOCK)[:, None] + BLOCK
    ki = jnp.arange(2 * BLOCK)[None, :]
    rel = qi - ki
    band = (rel >= 0) & (rel < WINDOW)
    blk = jnp.arange(nb)[:, None, None]
    valid = band[None] & ((blk > 0) | (ki >= BLOCK)[None])
    s = jnp.where(valid[None, :, None, None], s, -jnp.inf)
    sink = sinks.astype(jnp.float32).reshape(N_KV_HEADS, Q_PER_KV)[None, None, :, :, None, None]
    m = jnp.maximum(jnp.max(s, axis=-1, keepdims=True), sink)
    p = jnp.exp(s - m)
    denom = jnp.sum(p, axis=-1, keepdims=True) + jnp.exp(sink - m)
    w = (p / denom).astype(v.dtype)
    o = jnp.einsum('bngrqk,bnkgd->bnqgrd', w, vb)
    return o.reshape(B, T, N_Q_HEADS * HEAD_DIM)

def memory_cross_attention(q, k, v):
    B, T = q.shape[0], q.shape[1]
    s = jnp.einsum('bthd,bmhd->bhtm', q, k).astype(jnp.float32) * (HEAD_DIM ** -0.5)
    w = jax.nn.softmax(s, axis=-1).astype(v.dtype)
    o = jnp.einsum('bhtm,bmhd->bthd', w, v)
    return o.reshape(B, T, N_MEM_HEADS * HEAD_DIM)

def conformer_conv(u, w_dw, b_dw, g_ln, b_ln):
    a, gate = jnp.split(u, 2, axis=-1)
    h = a * jax.nn.sigmoid(gate)
    h = lax.conv_general_dilated(
        h, w_dw[:, None, :].astype(h.dtype), window_strides=(1,),
        padding=((CONV_WIDTH - 1, 0),), dimension_numbers=('NWC', 'WIO', 'NWC'),
        feature_group_count=CONV_CH) + b_dw
    return jax.nn.silu(layer_norm(h, g_ln, b_ln))

def first_inputs(seed: int = 0) -> dict:
    key = jax.random.key(seed)
    ks = jax.random.split(key, 32)
    f32 = jnp.float32

    def w(k, shape, fan_in):
        return jax.random.normal(k, shape, f32) * (fan_in ** -0.5)

    def gain(k, shape):
        return 1.0 + 0.05 * jax.random.normal(k, shape, f32)

    L = DEPTH
    start = jax.random.randint(ks[2], (BATCH, 1), 0, 1024, dtype=jnp.int32)
    positions = start + jnp.arange(SEQ, dtype=jnp.int32)[None, :]
    return {
        "x": jax.random.normal(ks[0], (BATCH, SEQ, D_MODEL), f32),
        "mem": jax.random.normal(ks[1], (BATCH, MEM_LEN, D_MODEL), f32),
        "positions": positions,
        "g_ffn1": gain(ks[3], (L, D_MODEL)),
        "w_ffn1_gate": w(ks[4], (L, D_MODEL, D_FF), D_MODEL),
        "w_ffn1_up": w(ks[5], (L, D_MODEL, D_FF), D_MODEL),
        "w_ffn1_down": w(ks[6], (L, D_FF, D_MODEL), D_FF),
        "g_mix": gain(ks[7], (L, D_MODEL)),
        "w_in": w(ks[8], (L, D_MODEL, IN_COLS), D_MODEL),
        "g_q": gain(ks[9], (L, HEAD_DIM)),
        "g_k": gain(ks[10], (L, HEAD_DIM)),
        "sinks": 0.5 * jax.random.normal(ks[11], (L, N_Q_HEADS), f32),
        "w_dw": w(ks[12], (L, CONV_WIDTH, CONV_CH), CONV_WIDTH),
        "b_dw": 0.02 * jax.random.normal(ks[13], (L, CONV_CH), f32),
        "g_conv_ln": gain(ks[14], (L, CONV_CH)),
        "b_conv_ln": 0.02 * jax.random.normal(ks[15], (L, CONV_CH), f32),
        "g_mem": gain(ks[16], (L, D_MODEL)),
        "w_mem_kv": w(ks[17], (L, D_MODEL, 2 * MQ_COLS), D_MODEL),
        "g_mq": gain(ks[18], (L, HEAD_DIM)),
        "g_mk": gain(ks[19], (L, HEAD_DIM)),
        "w_out": w(ks[20], (L, MIX_WIDTH, D_MODEL), MIX_WIDTH),
        "g_ffn2": gain(ks[21], (L, D_MODEL)),
        "w_ffn2_gate": w(ks[22], (L, D_MODEL, D_FF), D_MODEL),
        "w_ffn2_up": w(ks[23], (L, D_MODEL, D_FF), D_MODEL),
        "w_ffn2_down": w(ks[24], (L, D_FF, D_MODEL), D_FF),
    }

def first_block(x, mem, positions, g_ffn1, w_ffn1_gate, w_ffn1_up, w_ffn1_down,
              g_mix, w_in, g_q, g_k, sinks, w_dw, b_dw, g_conv_ln, b_conv_ln,
              g_mem, w_mem_kv, g_mq, g_mk, w_out,
              g_ffn2, w_ffn2_gate, w_ffn2_up, w_ffn2_down):
    B, T = x.shape[0], x.shape[1]
    M = mem.shape[1]
    for l in range(DEPTH):
        x = x + 0.5 * swiglu(rms_norm(x, g_ffn1[l]), w_ffn1_gate[l], w_ffn1_up[l], w_ffn1_down[l])

        h = rms_norm(x, g_mix[l])
        proj = h @ w_in[l]
        q, k, v, u, mq = jnp.split(proj, SPLITS, axis=-1)
        q = q.reshape(B, T, N_Q_HEADS, HEAD_DIM)
        k = k.reshape(B, T, N_KV_HEADS, HEAD_DIM)
        v = v.reshape(B, T, N_KV_HEADS, HEAD_DIM)
        q = rope_partial(rms_norm(q, g_q[l]), positions)
        k = rope_partial(rms_norm(k, g_k[l]), positions)
        y_attn = sliding_window_attention(q, k, v, sinks[l])

        y_conv = conformer_conv(u, w_dw[l], b_dw[l], g_conv_ln[l], b_conv_ln[l])

        mkv = rms_norm(mem, g_mem[l]) @ w_mem_kv[l]
        mk, mv = jnp.split(mkv, 2, axis=-1)
        mq = rms_norm(mq.reshape(B, T, N_MEM_HEADS, HEAD_DIM), g_mq[l])
        mk = rms_norm(mk.reshape(B, M, N_MEM_HEADS, HEAD_DIM), g_mk[l])
        mv = mv.reshape(B, M, N_MEM_HEADS, HEAD_DIM)
        y_mem = memory_cross_attention(mq, mk, mv)

        x = x + jnp.concatenate([y_attn, y_conv, y_mem], axis=-1) @ w_out[l]

        x = x + 0.5 * swiglu(rms_norm(x, g_ffn2[l]), w_ffn2_gate[l], w_ffn2_up[l], w_ffn2_down[l])
    return x


DEPTH_2 = 2

N_MIXERS = 2
N_HEADS = 16
N_KV_HEADS_2 = 4
GROUP = N_HEADS // N_KV_HEADS_2
IDX_HEADS = 8
IDX_DIM = 64
TOPK_MAX = 256
Q_BLOCK = 128
ROPE_THETA_2 = 10000.0
CONV_WIDTH_2 = 3
FFN_HIDDEN = int(math.ceil(8 * D_MODEL / 3 / 256) * 256)
NORM_EPS = 1e-6
N_A = (DEPTH_2 + 1) // 2
N_B = DEPTH_2 // 2

Q_COLS_2 = N_HEADS * HEAD_DIM
K_COLS = N_KV_HEADS_2 * HEAD_DIM
V_COLS = N_KV_HEADS_2 * HEAD_DIM
QI_COLS = IDX_HEADS * IDX_DIM
KI_COLS = IDX_DIM
WI_COLS = IDX_HEADS
ATTN_IN_COLS = Q_COLS_2 + K_COLS + V_COLS + QI_COLS + KI_COLS + WI_COLS


def _rmsnorm(x, g):
    xf = x.astype(jnp.float32)
    y = xf * lax.rsqrt(jnp.mean(xf * xf, axis=-1, keepdims=True) + NORM_EPS)
    return (y * g.astype(jnp.float32)).astype(x.dtype)

def _layernorm(x, g, b):
    xf = x.astype(jnp.float32)
    mu = jnp.mean(xf, axis=-1, keepdims=True)
    var = jnp.mean(jnp.square(xf - mu), axis=-1, keepdims=True)
    y = (xf - mu) * lax.rsqrt(var + NORM_EPS)
    return (y * g.astype(jnp.float32) + b.astype(jnp.float32)).astype(x.dtype)

def _rope(x, pos):
    d = x.shape[-1]
    half = d // 2
    inv_freq = ROPE_THETA_2 ** (-(jnp.arange(half, dtype=jnp.float32) * 2.0 / d))
    ang = pos.astype(jnp.float32)[..., None] * inv_freq
    cos = jnp.cos(ang)[:, :, None, :]
    sin = jnp.sin(ang)[:, :, None, :]
    xf = x.astype(jnp.float32)
    x1, x2 = xf[..., :half], xf[..., half:]
    out = jnp.concatenate([x1 * cos - x2 * sin, x2 * cos + x1 * sin], axis=-1)
    return out.astype(x.dtype)

def _dsa_mixer(h, positions, w_in, q_norm_g, k_norm_g, idx_k_ln_g, idx_k_ln_b, w_out):
    Bn, T, _ = h.shape
    proj = h @ w_in
    o0 = 0
    q = proj[..., o0:o0 + Q_COLS_2].reshape(Bn, T, N_HEADS, HEAD_DIM); o0 += Q_COLS_2
    k = proj[..., o0:o0 + K_COLS].reshape(Bn, T, N_KV_HEADS_2, HEAD_DIM); o0 += K_COLS
    v = proj[..., o0:o0 + V_COLS].reshape(Bn, T, N_KV_HEADS_2, HEAD_DIM); o0 += V_COLS
    qi = proj[..., o0:o0 + QI_COLS].reshape(Bn, T, IDX_HEADS, IDX_DIM); o0 += QI_COLS
    ki = proj[..., o0:o0 + KI_COLS]; o0 += KI_COLS
    wi = proj[..., o0:o0 + WI_COLS]

    q = _rope(_rmsnorm(q, q_norm_g), positions)
    k = _rope(_rmsnorm(k, k_norm_g), positions)
    qi = _rope(qi, positions)
    ki = _rope(_layernorm(ki, idx_k_ln_g, idx_k_ln_b)[:, :, None, :], positions)[:, :, 0, :]
    wi = wi * (IDX_HEADS ** -0.5 * IDX_DIM ** -0.5)

    topk = min(TOPK_MAX, T // 4)
    n_blk = T // Q_BLOCK
    key_idx = jnp.arange(T)
    scale = HEAD_DIM ** -0.5

    def to_blocks(a):
        return jnp.moveaxis(a.reshape(Bn, n_blk, Q_BLOCK, *a.shape[2:]), 1, 0)

    def block_fn(args):
        qb, qib, wib, start = args
        t_idx = start + jnp.arange(Q_BLOCK)
        s = jnp.einsum('bqhd,bsd->bqhs', qib, ki)
        score = jnp.einsum('bqhs,bqh->bqs', jax.nn.relu(s), wib).astype(jnp.float32)
        causal = key_idx[None, :] <= t_idx[:, None]
        score = jnp.where(causal[None], score, -jnp.inf)
        _, sel = lax.top_k(score, topk)
        sel_ok = sel <= t_idx[None, :, None]
        kg = jax.vmap(lambda a, i: a[i])(k, sel)
        vg = jax.vmap(lambda a, i: a[i])(v, sel)
        qg = qb.reshape(Bn, Q_BLOCK, N_KV_HEADS_2, GROUP, HEAD_DIM)
        logits = jnp.einsum('bqgrd,bqkgd->bqgrk', qg, kg).astype(jnp.float32) * scale
        logits = jnp.where(sel_ok[:, :, None, None, :], logits, -1e30)
        p = jax.nn.softmax(logits, axis=-1).astype(vg.dtype)
        o = jnp.einsum('bqgrk,bqkgd->bqgrd', p, vg)
        return o.reshape(Bn, Q_BLOCK, N_HEADS * HEAD_DIM)

    starts = jnp.arange(n_blk) * Q_BLOCK
    o = lax.map(block_fn, (to_blocks(q), to_blocks(qi), to_blocks(wi), starts))
    o = jnp.moveaxis(o, 0, 1).reshape(Bn, T, N_HEADS * HEAD_DIM)
    return o @ w_out

def _short_conv_mixer(h, w_in, conv_w, w_out):
    proj = h @ w_in
    b_gate, c_gate, u = jnp.split(proj, 3, axis=-1)
    z = c_gate * u
    z = lax.conv_general_dilated(
        z, conv_w[:, None, :].astype(z.dtype),
        window_strides=(1,), padding=[(CONV_WIDTH_2 - 1, 0)],
        dimension_numbers=('NWC', 'WIO', 'NWC'),
        feature_group_count=z.shape[-1])
    return (b_gate * z) @ w_out

def _swiglu(h, w_gate, w_up, w_down):
    return (jax.nn.silu(h @ w_gate) * (h @ w_up)) @ w_down

def second_inputs(seed: int = 0) -> dict:
    key = jax.random.key(seed)
    ks = jax.random.split(key, 20)
    D = D_MODEL

    def nrm(k, shape, s):
        return jax.random.normal(k, shape, dtype=jnp.float32) * s

    x = nrm(ks[0], (BATCH, SEQ, D), 1.0)
    c = nrm(ks[1], (BATCH, D), 1.0)
    positions = (jnp.arange(SEQ, dtype=jnp.int32)[None, :]
                 + jax.random.randint(ks[2], (BATCH, 1), 0, 1024, dtype=jnp.int32))
    ada_w = nrm(ks[3], (DEPTH_2, D, 6 * D), 0.5 * D ** -0.5)
    ada_b = nrm(ks[4], (DEPTH_2, 6 * D), 0.02)
    norm1_g = 1.0 + nrm(ks[5], (DEPTH_2, D), 0.02)
    norm2_g = 1.0 + nrm(ks[6], (DEPTH_2, D), 0.02)
    attn_w_in = nrm(ks[7], (N_A, D, ATTN_IN_COLS), D ** -0.5)
    attn_q_norm_g = 1.0 + nrm(ks[8], (N_A, HEAD_DIM), 0.02)
    attn_k_norm_g = 1.0 + nrm(ks[9], (N_A, HEAD_DIM), 0.02)
    idx_k_ln_g = 1.0 + nrm(ks[10], (N_A, IDX_DIM), 0.02)
    idx_k_ln_b = nrm(ks[11], (N_A, IDX_DIM), 0.02)
    attn_w_out = nrm(ks[12], (N_A, N_HEADS * HEAD_DIM, D), (N_HEADS * HEAD_DIM) ** -0.5)
    conv_w_in = nrm(ks[13], (N_B, D, 3 * D), D ** -0.5)
    conv_w = nrm(ks[14], (N_B, CONV_WIDTH_2, D), CONV_WIDTH_2 ** -0.5)
    conv_w_out = nrm(ks[15], (N_B, D, D), D ** -0.5)
    ffn_w_gate = nrm(ks[16], (DEPTH_2, D, FFN_HIDDEN), D ** -0.5)
    ffn_w_up = nrm(ks[17], (DEPTH_2, D, FFN_HIDDEN), D ** -0.5)
    ffn_w_down = nrm(ks[18], (DEPTH_2, FFN_HIDDEN, D), FFN_HIDDEN ** -0.5)
    return {"x": x, "c": c, "positions": positions,
            "ada_w": ada_w, "ada_b": ada_b, "norm1_g": norm1_g, "norm2_g": norm2_g,
            "attn_w_in": attn_w_in, "attn_q_norm_g": attn_q_norm_g,
            "attn_k_norm_g": attn_k_norm_g, "idx_k_ln_g": idx_k_ln_g,
            "idx_k_ln_b": idx_k_ln_b, "attn_w_out": attn_w_out,
            "conv_w_in": conv_w_in, "conv_w": conv_w, "conv_w_out": conv_w_out,
            "ffn_w_gate": ffn_w_gate, "ffn_w_up": ffn_w_up, "ffn_w_down": ffn_w_down}

def second_block(x, c, positions, ada_w, ada_b, norm1_g, norm2_g,
              attn_w_in, attn_q_norm_g, attn_k_norm_g, idx_k_ln_g, idx_k_ln_b, attn_w_out,
              conv_w_in, conv_w, conv_w_out, ffn_w_gate, ffn_w_up, ffn_w_down):
    c_act = jax.nn.silu(c)
    for i in range(DEPTH_2):
        mod = c_act @ ada_w[i] + ada_b[i]
        sh1, sc1, g1, sh2, sc2, g2 = [m[:, None, :] for m in jnp.split(mod, 6, axis=-1)]
        h = _rmsnorm(x, norm1_g[i]) * (1.0 + sc1) + sh1
        if i % N_MIXERS == 0:
            j = i // N_MIXERS
            y = _dsa_mixer(h, positions, attn_w_in[j], attn_q_norm_g[j], attn_k_norm_g[j],
                           idx_k_ln_g[j], idx_k_ln_b[j], attn_w_out[j])
        else:
            j = i // N_MIXERS
            y = _short_conv_mixer(h, conv_w_in[j], conv_w[j], conv_w_out[j])
        x = x + g1 * y
        h = _rmsnorm(x, norm2_g[i]) * (1.0 + sc2) + sh2
        x = x + g2 * _swiglu(h, ffn_w_gate[i], ffn_w_up[i], ffn_w_down[i])
    return x


def setup_inputs(seed=0):
    out = dict(first_inputs(seed))
    for name, value in second_inputs(seed + 1).items():
        if name != "x":
            out[name + "_2"] = value
    return out


def reference(
    x, mem, positions, g_ffn1, w_ffn1_gate, w_ffn1_up, w_ffn1_down, g_mix, w_in, g_q, g_k,
    sinks, w_dw, b_dw, g_conv_ln, b_conv_ln, g_mem, w_mem_kv, g_mq, g_mk, w_out, g_ffn2,
    w_ffn2_gate, w_ffn2_up, w_ffn2_down, c_2, positions_2, ada_w_2, ada_b_2, norm1_g_2,
    norm2_g_2, attn_w_in_2, attn_q_norm_g_2, attn_k_norm_g_2, idx_k_ln_g_2, idx_k_ln_b_2,
    attn_w_out_2, conv_w_in_2, conv_w_2, conv_w_out_2, ffn_w_gate_2, ffn_w_up_2, ffn_w_down_2,
):
    x = first_block(
        x, mem, positions, g_ffn1, w_ffn1_gate, w_ffn1_up, w_ffn1_down, g_mix, w_in, g_q, g_k,
        sinks, w_dw, b_dw, g_conv_ln, b_conv_ln, g_mem, w_mem_kv, g_mq, g_mk, w_out, g_ffn2,
        w_ffn2_gate, w_ffn2_up, w_ffn2_down,
    )
    return second_block(
        x, c_2, positions_2, ada_w_2, ada_b_2, norm1_g_2, norm2_g_2, attn_w_in_2,
        attn_q_norm_g_2, attn_k_norm_g_2, idx_k_ln_g_2, idx_k_ln_b_2, attn_w_out_2, conv_w_in_2,
        conv_w_2, conv_w_out_2, ffn_w_gate_2, ffn_w_up_2, ffn_w_down_2,
    )


_drawn_inputs = setup_inputs


def setup_inputs(seed=0):
    import zlib

    import numpy as np

    out = dict(_drawn_inputs(seed))
    spreads = {}
    factors = {'g_q': 7.972,
     'g_k': 7.877,
     'sinks': 64.0,
     'b_dw': 3.859,
     'g_conv_ln': 2.918,
     'b_conv_ln': 8.0,
     'g_mem': 8.0,
     'g_mq': 8.0,
     'g_mk': 8.0,
     'norm1_g_2': 4.602,
     'norm2_g_2': 7.299,
     'attn_q_norm_g_2': 8.0,
     'attn_k_norm_g_2': 8.0,
     'idx_k_ln_g_2': 8.0,
     'idx_k_ln_b_2': 8.0}
    for name, (base, spread) in spreads.items():
        noise = np.random.default_rng([zlib.crc32(name.encode()), seed]).standard_normal(out[name].shape)
        drawn = base * np.exp(spread * noise) if base else spread * noise
        out[name] = __import__('jax').numpy.asarray(drawn.astype(out[name].dtype))
    for name, factor in factors.items():
        out[name] = (out[name] * factor).astype(out[name].dtype)
    return out
```

```python
from contextlib import ExitStack
import math

import numpy as np

import concourse.bass as bass
from concourse import mybir

ALU = mybir.AluOpType
ACT = mybir.ActivationFunctionType
F32 = mybir.dt.float32
F32R = mybir.dt.float32r
I32 = mybir.dt.int32
AX_X = mybir.AxisListType.X

P = 128
T = 512
D = 1024
KC = D // P
FF = 2816
FC = FF // P
M = 256
TT = T // P
MT = M // P
HD = 64
RING = 4
LEAD = 2
WT = KC * P
DOWN_CUTS = (0, 6, 12, 17, 22)
UP_JOBS = 2 * FC
DOWN_JOBS = 4 * KC
ADA = 512
ADA_STEPS = 2 * 6 * D // ADA
ADA_PER_FFN = 8
CONV_A = 31
CONV_B = 3
PAD_A = CONV_A - 1
PAD_B = CONV_B - 1
TOPK = 128
ROUNDS = TOPK // 8
EPS = 1e-6
SCALE = HD ** -0.5
MASKED = -1e30
TAKEN = -3e38
NO_SINK = -3e38
WI_SCALE = 8 ** -0.5 * HD ** -0.5
TWO_PI = 2 * math.pi
PI_A = 6.28125
PI_B = float(np.float32(np.round((TWO_PI - PI_A) * 2 ** 21) / 2 ** 21))
PI_C = float(np.float32(TWO_PI - PI_A - PI_B))
ROUNDER = 1.5 * 2 ** 23
PI_CLAMP = 3.1415925

COLS = {}
_at = 0
for _name, _n in (("g_ffn1", KC), ("g_mix", KC), ("g_ffn2", KC), ("n1_0", KC), ("n2_0", KC), ("n1_1", KC),
                  ("n2_1", KC), ("g_mem", KC), ("g_q", 1), ("g_k", 1), ("g_mq", 1), ("g_mk", 1), ("g_q2", 1),
                  ("g_k2", 1), ("ln_g", 1), ("ln_b", 1), ("b_dw", 2), ("cln_g", 2), ("cln_b", 2), ("w_dw", 2 * CONV_A),
                  ("sinks", 8), ("conv_w", KC * CONV_B), ("c", KC), ("ada_b", 2 * 6 * KC), ("freq_a", 1), ("freq_b", 1)):
    COLS[_name] = (_at, _n)
    _at += _n
NCOLS = _at
MATS = {"ident": (0, P), "heads": (P, P), "pair_a": (2 * P, P), "pair_b": (3 * P, P), "mask": (4 * P, 2 * P)}
NMATS = 6 * P


class Marks:

    def __init__(self, sem, keys):
        self.sem, self.keys, self.given = sem, list(keys), 0
        self.value = {k: n + 1 for n, k in enumerate(self.keys)}
        assert len(self.value) == len(self.keys)

    def at(self, key):
        assert self.keys[self.given] == key, (key, self.keys[self.given])
        self.given += 1
        return self.sem


def build(nc, A, out):
    ctx = ExitStack()
    with ctx:
        def sem(name):
            return ctx.enter_context(nc.semaphore(name))

        def keep(name, cols, dt=F32):
            return ctx.enter_context(nc.sbuf_tensor(name, [P, cols], dt))

        x = keep("x", KC * T)
        h_hi = keep("h_hi", KC * T, F32R)
        h_lo = keep("h_lo", KC * T, F32R)
        w_raw = keep("w_raw", RING * WT)
        w_hi = keep("w_hi", RING * WT, F32R)
        w_lo = keep("w_lo", RING * WT, F32R)
        tmp = keep("tmp", 4 * T)
        ssum = keep("ssum", T)
        ada_raw = keep("ada_raw", 2 * 2 * ADA)
        ada_sum = keep("ada_sum", ADA)
        ones = keep("ones", P)
        cols = keep("cols", NCOLS)
        modc = keep("modc", 2 * 6 * KC)
        c_act = keep("c_act", KC)
        geff = keep("geff", 4 * KC)
        flat = keep("flat", 3 * KC)
        tiny = keep("tiny", 2)
        sink8 = keep("sink8", 8)
        small = keep("small", 4 * 4)
        top8 = keep("top8", 8)
        wi = keep("wi", TT * 8)
        ps = ctx.enter_context(nc.psum_tensor("ps", [P, 8 * T], F32))

        def stage_memory(wanted):
            with ExitStack() as s:
                return [s.enter_context(nc.sbuf_tensor(n, [P, c], dt)) for n, c, dt in wanted]

        hid_hi, hid_lo = stage_memory([("hid_hi", FC * T, F32R), ("hid_lo", FC * T, F32R)])
        (matsA, memx, mh_hi, mh_lo, qA, kA, vA, mq, mk, mv, cosA, sinA, glu, conv, sig, smA, pA, pTA, qnA, hsA, hrA,
         ropA, zeroA) = stage_memory([
            ("matsA", NMATS, F32), ("memx", KC * M, F32), ("mh_hi", KC * M, F32R), ("mh_lo", KC * M, F32R),
            ("qA", 4 * T, F32), ("kA", T, F32), ("vA", TT * P, F32), ("mq", 2 * T, F32), ("mk", 2 * M, F32),
            ("mv", 2 * MT * P, F32), ("cosA", T, F32), ("sinA", T, F32), ("glu", 2 * (PAD_A + T), F32),
            ("conv", 2 * T, F32), ("sig", T, F32), ("smA", 2 * (M + 8), F32), ("pA", 3 * (M + 8), F32),
            ("pTA", 2 * M, F32), ("qnA", 2 * T, F32), ("hsA", 2 * T, F32), ("hrA", T, F32), ("ropA", 2 * T, F32),
            ("zeroA", M, F32)])
        (matsB, qB, kB, vB, qi, ki, cosB, sinB, dmask, score, relu, smB, pB, pTB, qnB, hsB, hrB, ropB, kraw) = \
            stage_memory([
                ("matsB", NMATS, F32), ("qB", 8 * T, F32), ("kB", 2 * T, F32), ("vB", TT * 2 * P, F32),
                ("qi", 4 * T, F32), ("ki", T, F32), ("cosB", T, F32), ("sinB", T, F32), ("dmask", 9 * P, F32),
                ("score", 9 * P, F32), ("relu", 2 * T, F32), ("smB", 2 * T, F32), ("pB", 3 * T, F32),
                ("pTB", 2 * T, F32), ("qnB", 2 * T, F32), ("hsB", 2 * T, F32), ("hrB", T, F32), ("ropB", 2 * T, F32),
                ("kraw", T, F32)])
        zc, c_sb, tap, y_hi, y_lo = stage_memory([
            ("zc", 2 * (PAD_B + T), F32), ("c_sb", 2 * T, F32), ("tap", 2 * T, F32), ("y_hi", KC * T, F32R),
            ("y_lo", KC * T, F32R)])

        def bank(n):
            return ps[:, n * T:(n + 1) * T]

        def chunk(t, k, width=T):
            return t[:, k * width:(k + 1) * width]

        def col(name, n=0, count=1):
            at = COLS[name][0] + n
            return cols[:, at:at + count]

        def f32(ap):
            return ap.bitcast(F32)

        UNITS_A = [("win", j, b, half) for j in range(4) for b in range(TT) for half in range(2)]
        UNITS_A += [("mem", j, b, half) for j in range(2) for b in range(TT) for half in range(2)]
        UNITS_B = [("dsa", j, b, half) for j in range(8) for b in range(TT) for half in range(2)]
        TILES_A = ["vA", "kA", "qA0", "qA1", "qA2", "qA3", "g0", "a0", "g1", "a1", "mq0", "mq1",
                   "mk0", "mk1", "mv0", "mv1"]
        TILES_B = ["ki", "wi", "qi0", "qi1", "qi2", "qi3", "vB0", "vB1", "kB0", "kB1"] + [f"qB{t}" for t in range(8)]
        first_job, at = {}, 0
        for stage, count in (("ffn0", UP_JOBS + DOWN_JOBS), ("mixA", len(TILES_A)), ("outA", KC),
                             ("ffn1", UP_JOBS + DOWN_JOBS), ("mixB", len(TILES_B)), ("outB", KC),
                             ("ffn2", UP_JOBS + DOWN_JOBS), ("mixC", 3 * KC), ("outC", KC),
                             ("ffn3", UP_JOBS + DOWN_JOBS)):
            first_job[stage] = at
            at += count
        JOBS = at
        WEIGHTS = {"outA": "w_out", "outB": "w_out_b", "outC": "w_out_c", "mixA": "w_mix", "mixB": "w_mix_b",
                   "mixC": "w_mix_c"}

        consts_in = sem("consts_in")
        x_in = sem("x_in")
        stage_in = sem("stage_in")
        w_in = [sem(f"w_in{s}") for s in range(RING)]
        w_hi_done = sem("w_hi_done")
        w_lo_done = sem("w_lo_done")
        job_done = sem("job_done")
        silu_done = sem("silu_done")
        hid_done = sem("hid_done")
        hid_hi_done = sem("hid_hi_done")
        hid_lo_done = sem("hid_lo_done")
        x_done = sem("x_done")
        sq_done = sem("sq_done")
        ss_done = sem("ss_done")
        total_done = sem("total_done")
        std_done = sem("std_done")
        rstd_done = sem("rstd_done")
        normed = sem("normed")
        h_hi_done = sem("h_hi_done")
        h_lo_done = sem("h_lo_done")
        ada_in = [sem(f"ada_in{s}") for s in range(2)]
        ada_sum_done = sem("ada_sum_done")
        ada_mm_done = sem("ada_mm_done")
        ada_done = sem("ada_done")
        c_done = sem("c_done")
        z_done = sem("z_done")
        tap_done = sem("tap_done")
        y_done = sem("y_done")
        y_hi_done = sem("y_hi_done")
        y_lo_done = sem("y_lo_done")
        out_done = sem("out_done")
        prep = sem("prep")

        def has_norm(t):
            return t[:2] in ("kA", "qA", "mq", "mk", "kB", "qB", "ki")

        def has_rope(t):
            return t[:2] in ("kA", "qA", "kB", "qB", "ki", "qi")

        def is_token_major(t):
            return t[:2] in ("vA", "mv", "vB", "wi")

        HEADS = [t for t in TILES_A + TILES_B if has_norm(t) or has_rope(t)]
        NORMS = [t for t in HEADS if has_norm(t)]
        ROPES = [t for t in HEADS if has_rope(t)]
        def in_step_order(tiles, late):
            keyed = []
            for t in tiles:
                lists = TILES_A if t in TILES_A else TILES_B
                keyed.append((lists is TILES_B, lists.index(t) + (late if t == "ki" else 0), t))
            return [t for _, _, t in sorted(keyed, key=lambda k: k[:2])]

        h_sq = Marks(sem("h_sq"), in_step_order(NORMS, 1.5))
        h_sum = Marks(sem("h_sum"), in_step_order(NORMS, 1.5))
        h_std = Marks(sem("h_std"), in_step_order(NORMS, 1.5))
        h_rstd = Marks(sem("h_rstd"), in_step_order(NORMS, 1.5))
        h_normed = Marks(sem("h_normed"), in_step_order(HEADS, 1.5))
        h_rot = Marks(sem("h_rot"), in_step_order(ROPES, 1.5))
        h_sin = Marks(sem("h_sin"), in_step_order(ROPES, 1.5))
        h_roped = Marks(sem("h_roped"), in_step_order(ROPES, 1.5))
        evac = Marks(sem("evac"), [t for t in TILES_A + TILES_B if is_token_major(t) or t == "ki" or t[0] == "g"])
        glu_done = Marks(sem("glu_done"), ["a0", "a1"])

        UNITS = UNITS_A + UNITS_B
        u_score = Marks(sem("u_score"), UNITS)
        u_masked = Marks(sem("u_masked"), UNITS)
        u_negmax = Marks(sem("u_negmax"), UNITS)
        u_exp = Marks(sem("u_exp"), UNITS)
        u_inv = Marks(sem("u_inv"), UNITS)
        u_prob = Marks(sem("u_prob"), UNITS)
        u_turned = Marks(sem("u_turned"), UNITS)
        u_pt = Marks(sem("u_pt"), UNITS)
        u_out = Marks(sem("u_out"), UNITS)
        GROUPS = [("win", j) for j in range(4)] + [("mem", j) for j in range(2)] + [("dsa", j) for j in range(8)]
        g_hi = Marks(sem("g_hi"), ["c0", "c1"] + GROUPS)
        g_lo = Marks(sem("g_lo"), ["c0", "c1"] + GROUPS)
        IDX = [(b, h) for b in range(1, TT) for h in range(8)]
        i_score = Marks(sem("i_score"), IDX)
        i_relu = Marks(sem("i_relu"), IDX)
        i_sum = Marks(sem("i_sum"), IDX)
        TOPS = []
        for b in range(1, TT):
            TOPS += [(b, "tri")] + [(b, r, s) for r in range(ROUNDS) for s in ("max", "take")] + [(b, "mask")]
        top = Marks(sem("top"), TOPS)

        TAB = ["ang", "turns", "whole", "r1", "r2", "r3", "clamp"]
        d_misc = Marks(sem("d_misc"),
                       [("tabA", s) for s in ["pos"] + TAB] + ["mem_sum", "mem_rstd"] +
                       [("mem", k) for k in range(KC)] + ["mem_lo"] +
                       [("conv", t, c) for t in range(CONV_A) for c in range(2)] +
                       ["ctr0", "ctr1", "conv_rstd", "conv_n0", "conv_n1", "geff0", "geff1"] +
                       [("tabB", s) for s in ["pos"] + TAB] + ["ki_ctr", "ki_g", "geff2", "geff3"])
        a_misc = Marks(sem("a_misc"),
                       ["sink8", ("tabA", "sin"), ("tabA", "abs"), ("tabA", "cos"), "mem_sq", "mem_std", "mem_hi",
                        "conv_sq0", "conv_sq1", "conv_std", "conv_y0", "conv_y1",
                        ("tabB", "sin"), ("tabB", "abs"), ("tabB", "cos")])
        p_misc = Marks(sem("p_misc"), ["mem_total", "conv_total", "conv_var", "ki_total"])

        def after(eng, marks, key):
            eng.wait_ge(marks.sem, marks.value[key])

        def after_nth(eng, marks, n):
            if n >= 0:
                eng.wait_ge(marks.sem, n + 1)

        block = ctx.enter_context(nc.Block())


        @block.sync
        def _(sp):
            def load(first, i, step, src):
                slot, width = first % RING, src.shape[-1]
                sp.wait_ge(w_lo_done, i * step + (first + 1))
                sp.dma_start(w_raw[:, slot * WT:slot * WT + width], src).then_inc(w_in[slot], 16)

            def tile_of(w, n):
                return A[w][bass.ds(n, 1), :, :].rearrange("a p n -> (a p) n")

            def ffn(n):
                J = first_job[f"ffn{n}"]

                with sp.Fori(0, FC // 2) as i:
                    for s in range(4):
                        load(J + s, i, 4, tile_of(f"{('gate', 'up')[s % 2]}{n}", i * 2 + s // 2))
                with sp.Fori(0, KC) as j:
                    for s in range(4):
                        load(J + UP_JOBS + s, j, 4,
                             A[f"down{n}"][bass.ds(j, 1), :, DOWN_CUTS[s] * P:DOWN_CUTS[s + 1] * P]
                             .rearrange("a p n -> (a p) n"))

            def project(stage, count):
                J = first_job[stage]
                with sp.Fori(0, count // 4) as i:
                    for s in range(4):
                        load(J + s, i, 4, tile_of(WEIGHTS[stage], i * 4 + s))

            sp.dma_start(cols[:, :], A["cols"]).then_inc(consts_in, 16)
            for k in range(KC):
                sp.dma_start(chunk(x, k), A["x"][k]).then_inc(x_in, 16)
            ffn(0)
            project("mixA", len(TILES_A))
            project("outA", KC)
            ffn(1)
            J = first_job["mixB"]
            for t, name in enumerate(TILES_B):
                width = KC * 8 if name == "wi" else WT
                load(J + t, 0, 4, A["w_mix_b"][t, :, 0:width])
            project("outB", KC)
            ffn(2)
            project("mixC", 3 * KC)
            project("outC", KC)
            ffn(3)
            for j in range(KC):
                sp.wait_ge(x_done, 8 * 7 + j + 1)
                sp.dma_start(out[j], chunk(x, j)).then_inc(out_done, 16)
            sp.wait_ge(out_done, 16 * KC)

        @block.gpsimd
        def _(pool):
            def ada_load(n, piece):
                pool.wait_ge(ada_sum_done, n * 8 + (2 * piece + 2))
                src = A["ada_w"][bass.ds(n, 1), :, piece * 2 * ADA:(piece + 1) * 2 * ADA]
                pool.dma_start(ada_raw[:, (piece % 2) * 2 * ADA:(piece % 2 + 1) * 2 * ADA],
                             src.rearrange("a p n -> (a p) n")).then_inc(ada_in[piece % 2], 16)

            def ada_steps(n):
                with pool.Fori(n * ADA_PER_FFN, (n + 1) * ADA_PER_FFN) as a:
                    for piece in range(4):
                        ada_load(a, piece)

            ada_steps(0)
            pool.wait_ge(x_done, 16)
            pool.dma_start(memx[:, :], A["mem"]).then_inc(stage_in, 16)
            pool.dma_start(matsA[:, :], A["mats"]).then_inc(stage_in, 16)
            pool.dma_start(ropA[:, 0:T].bitcast(I32), A["positions"]).then_inc(stage_in, 16)
            ada_steps(1)
            pool.wait_ge(x_done, 32)
            pool.dma_start(matsB[:, :], A["mats"]).then_inc(stage_in, 16)
            pool.dma_start(ropB[:, 0:T].bitcast(I32), A["positions_2"]).then_inc(stage_in, 16)
            ada_steps(2)

        @block.tensor
        def _(pe):
            def product(ready, dest, pairs, first, last):
                for n, ((s_hi, s_lo), (m_hi, m_lo)) in enumerate(pairs):
                    if ready:
                        ready(n)
                    pe.matmul(dest, s_hi, m_hi, start=first and n == 0, stop=False)
                    pe.matmul(dest, s_hi, m_lo, start=False, stop=False)
                    mm = pe.matmul(dest, s_lo, m_hi, start=False, stop=last and n == len(pairs) - 1)
                return mm

            def weights(first, k, width=P):
                at = (first % RING) * WT + k * width
                return w_hi[:, at:at + width], w_lo[:, at:at + width]

            def take(first, i=0, step=4):
                pe.wait_ge(w_lo_done, i * step + (first + 1 + RING))

            def moving(k, lo=0, width=T):
                return h_hi[:, k * T + lo:k * T + lo + width], h_lo[:, k * T + lo:k * T + lo + width]

            def norm_total(n):
                pe.wait_ge(ss_done, 9 * (n + 1))
                pe.matmul(bank(6), ones[:, :], ssum[:, :], start=True, stop=True).then_inc(total_done, 1)

            def ffn(n):
                norm_total({0: 0, 1: 2, 2: 4, 3: 6}[n])
                J = first_job[f"ffn{n}"]
                N = {0: 0, 1: 2, 2: 4, 3: 6}[n]

                def up(i, modulation):
                    for s in range(4):
                        if s % 2 == 0:
                            pe.wait_ge(hid_done, i * 2 + (n * FC + s // 2 + 1))
                        take(J + s, i)
                        ready = (lambda k: pe.wait_ge(h_lo_done, N * KC + k + 1)) if s == 0 else None
                        product(ready, bank(s), [(weights(J + s, k), moving(k)) for k in range(KC)], True, True)\
                            .then_inc(job_done, 1)
                    if modulation:
                        a = i + n * ADA_PER_FFN
                        pe.wait_ge(ada_sum_done, a * 8 + 12)
                        pe.wait_ge(ada_done, a + 1)
                        for q in range(ADA // P):
                            mm = pe.matmul(bank(7)[:, q:q + 1], ada_sum[:, q * P:(q + 1) * P], ones[:, 0:1],
                                           start=True, stop=True)
                        mm.then_inc(ada_mm_done, 1)

                def down(i):
                    for s in range(8):
                        tile, part = s // 4, s % 4
                        js = J + UP_JOBS + s
                        if part == 0:
                            pe.wait_ge(hid_lo_done, (n + 1) * FC + 2)
                            pe.wait_ge(x_done, i * 2 + (8 * (2 * n + 1) + tile - 1))
                        take(js, i, 8)
                        c0, c1 = DOWN_CUTS[part], DOWN_CUTS[part + 1]
                        product(None, bank(4 + tile),
                                [(weights(js, c - c0), (chunk(hid_hi, c), chunk(hid_lo, c))) for c in range(c0, c1)],
                                part == 0, part == 3).then_inc(job_done, 1)

                if n < 3:
                    with pe.Fori(0, ADA_PER_FFN) as i:
                        up(i, True)
                with pe.Fori(ADA_PER_FFN if n < 3 else 0, FC // 2) as i:
                    up(i, False)
                with pe.Fori(0, KC // 2) as i:
                    down(i)

            def project(stage, r, ready_sem, ready, hi=h_hi, lo=h_lo):
                J = first_job[stage]
                with pe.Fori(0, KC // 4) as i:
                    for s in range(4):
                        if s == 0:
                            pe.wait_ge(ready_sem, ready)
                        pe.wait_ge(x_done, i * 4 + (8 * r + s - 3))
                        take(J + s, i)
                        product(None, bank(s), [(weights(J + s, k), (chunk(hi, k), chunk(lo, k))) for k in range(KC)],
                                True, True)\
                            .then_inc(job_done, 1)

            def freed(tiles, m):
                if m < 4:
                    return
                t = tiles[m - 4]
                if is_token_major(t) or t == "ki" or t[0] == "g":
                    after(pe, evac, t)
                elif t[0] == "a":
                    after(pe, glu_done, t)
                else:
                    after(pe, h_normed, t)

            def tile_job(tiles, stage, m, n_norm):
                t, js = tiles[m], first_job[stage] + m
                freed(tiles, m)
                take(js)
                ready = (lambda k: pe.wait_ge(h_lo_done, n_norm * KC + k + 1)) if m == 0 else None
                dest = bank(m % 4)
                if t[:2] in ("mk", "mv"):
                    after(pe, d_misc, "mem_lo")
                    if t[:2] == "mk":
                        mm = product(None, dest[:, 0:M], [(weights(js, k), (chunk(mh_hi, k, M), chunk(mh_lo, k, M)))
                                                          for k in range(KC)], True, True)
                    else:
                        for q in range(MT):
                            mm = product(None, dest[:, q * P:(q + 1) * P],
                                         [((mh_hi[:, k * M + q * P:k * M + (q + 1) * P],
                                            mh_lo[:, k * M + q * P:k * M + (q + 1) * P]), weights(js, k))
                                          for k in range(KC)], True, True)
                elif is_token_major(t):
                    width = 8 if t == "wi" else P
                    for q in range(TT):
                        mm = product(ready if q == 0 else None, dest[:, q * width:(q + 1) * width],
                                     [(moving(k, q * P, P), weights(js, k, width)) for k in range(KC)], True, True)
                else:
                    mm = product(ready, dest, [(weights(js, k), moving(k)) for k in range(KC)], True, True)
                mm.then_inc(job_done, 1)

            def head_sum(t, mats):
                after(pe, h_sq, t)
                n = h_sq.value[t] - 1
                after_nth(pe, h_std, n - 1)
                W = M if t[:2] == "mk" else T
                pe.matmul(bank(4)[:, 0:W], mats[:, P:2 * P], (hsA if mats is matsA else hsB)[:, (n % 2) * T:(n % 2) * T + W],
                          start=True, stop=True).then_inc(h_sum.at(t), 1)

            def head_turn(t, mats, which, qn):
                after(pe, h_normed, t)
                n = h_rot.value[t] - 1
                after_nth(pe, h_sin, n - 1)
                at = MATS[which][0]
                pe.matmul(bank(5), mats[:, at:at + P], chunk(qn, n % 2), start=True, stop=True)\
                    .then_inc(h_rot.at(t), 1)

            def attention(units, sc, tr, pv):
                for u in range(len(units) + 3):
                    if u < len(units):
                        sc(units[u])
                    if 2 <= u < len(units) + 2:
                        tr(units[u - 2])
                    if u >= 3:
                        pv(units[u - 3])

            def unit_score(unit, q, k, n):
                U = UNITS.index(unit)
                after_nth(pe, u_masked, U - 2)
                pe.matmul(bank(U % 2)[:, 0:n], q, k, start=True, stop=True).then_inc(u_score.at(unit), 1)

            def unit_turn(unit, p, width, mats, n):
                U = UNITS.index(unit)
                after(pe, u_prob, unit)
                after_nth(pe, u_pt, U - 2)
                for c in range(n // P):
                    mm = pe.transpose(bank(2 + U % 2)[:, c * P:(c + 1) * P],
                                      p[:, (U % 3) * width + c * P:(U % 3) * width + (c + 1) * P], mats[:, 0:P])
                mm.then_inc(u_turned.at(unit), 1)

            def unit_values(unit, pT, width, vs):
                kind, j, b, half = unit
                U = UNITS.index(unit)
                after(pe, u_pt, unit)
                G = GROUPS.index((kind, j))
                if b == 0 and half == 0 and G >= 2:
                    after(pe, g_lo, GROUPS[G - 2])
                dest = bank(4 + G % 2)[half * HD:(half + 1) * HD, b * P:(b + 1) * P]
                for c, v in enumerate(vs):
                    mm = pe.matmul(dest, v, pT[:, (U % 2) * width + c * P:(U % 2) * width + (c + 1) * P],
                                   start=c == 0, stop=c == len(vs) - 1)
                mm.then_inc(u_out.at(unit), 1)

            pe.wait_ge(prep, 1)
            ffn(0)

            norm_total(1)
            pe.wait_ge(stage_in, 48)
            for m in range(len(TILES_A) + 2):
                if m < len(TILES_A):
                    tile_job(TILES_A, "mixA", m, 1)
                if m >= 1 and m - 1 < len(TILES_A) and has_norm(TILES_A[m - 1]):
                    head_sum(TILES_A[m - 1], matsA)
                if m >= 2 and has_rope(TILES_A[m - 2]):
                    head_turn(TILES_A[m - 2], matsA, "pair_a", qnA)
                if m == 4:
                    after(pe, d_misc, "mem_sum")
                    pe.matmul(bank(6)[:, 0:M], ones[:, :], ssum[:, 0:M], start=True, stop=True)\
                        .then_inc(p_misc.at("mem_total"), 1)
            after(pe, d_misc, ("conv", CONV_A - 1, 1))
            for c in range(2):
                mm = pe.matmul(bank(6), ones[:, :], chunk(conv, c), start=c == 0, stop=c == 1)
            mm.then_inc(p_misc.at("conv_total"), 1)
            after(pe, a_misc, "conv_sq1")
            for c in range(2):
                mm = pe.matmul(bank(7), ones[:, :], chunk(hsA, c), start=c == 0, stop=c == 1)
            mm.then_inc(p_misc.at("conv_var"), 1)

            def scoreA(unit):
                kind, j, b, half = unit
                rows = slice(half * HD, (half + 1) * HD)
                if kind == "win":
                    n, lo = (P, 0) if b == 0 else (2 * P, (b - 1) * P)
                    unit_score(unit, qA[rows, j * T + b * P:j * T + (b + 1) * P], kA[rows, lo:lo + n], n)
                else:
                    unit_score(unit, mq[rows, j * T + b * P:j * T + (b + 1) * P], mk[rows, j * M:(j + 1) * M], M)

            def turnA(unit):
                unit_turn(unit, pA, M + 8, matsA, P if unit[0] == "win" and unit[2] == 0 else 2 * P)

            def valuesA(unit):
                kind, j, b, half = unit
                if kind == "win":
                    tiles = [b] if b == 0 else [b - 1, b]
                    vs = [vA[:, q * P + half * HD:q * P + (half + 1) * HD] for q in tiles]
                else:
                    vs = [mv[:, (j * MT + q) * P + half * HD:(j * MT + q) * P + (half + 1) * HD] for q in range(MT)]
                unit_values(unit, pTA, M, vs)

            after(pe, h_roped, "qA3")
            after(pe, h_normed, "mk1")
            after(pe, evac, "mv1")
            attention(UNITS_A, scoreA, turnA, valuesA)
            project("outA", 2, g_lo.sem, g_lo.value[("mem", 1)])
            ffn(1)

            norm_total(3)
            pe.wait_ge(stage_in, 80)
            for m in range(len(TILES_B) + 2):
                if m < len(TILES_B):
                    tile_job(TILES_B, "mixB", m, 3)
                if m == 1:
                    after(pe, evac, "ki")
                    pe.matmul(bank(6), matsB[:, P:2 * P], kraw[:, :], start=True, stop=True)\
                        .then_inc(p_misc.at("ki_total"), 1)
                if m == 2:
                    head_sum("ki", matsB)
                if 2 <= m <= len(TILES_B) and has_norm(TILES_B[m - 1]):
                    head_sum(TILES_B[m - 1], matsB)
                if m == 3:
                    head_turn("ki", matsB, "pair_b", qnB)
                if m >= 3 and has_rope(TILES_B[m - 2]):
                    head_turn(TILES_B[m - 2], matsB, "pair_b", qnB)
                if 8 <= m <= 10:
                    b = m - 7
                    n = (b + 1) * P
                    if b == 1:
                        after(pe, h_roped, "qi3")
                    for h in range(8):
                        I = IDX.index((b, h))
                        after_nth(pe, i_relu, I - 2)
                        rows = slice((h % 2) * HD, (h % 2 + 1) * HD)
                        pe.matmul(bank(6 + I % 2)[:, 0:n], qi[rows, (h // 2) * T + b * P:(h // 2) * T + (b + 1) * P],
                                  ki[rows, 0:n], start=True, stop=True).then_inc(i_score.at((b, h)), 1)

            def scoreB(unit):
                _, j, b, half = unit
                rows = slice(half * HD, (half + 1) * HD)
                n = (b + 1) * P
                unit_score(unit, qB[rows, j * T + b * P:j * T + (b + 1) * P],
                           kB[rows, (j // 4) * T:(j // 4) * T + n], n)

            def turnB(unit):
                unit_turn(unit, pB, T, matsB, (unit[2] + 1) * P)

            def valuesB(unit):
                _, j, b, half = unit
                at = (j // 4) * P + half * HD
                unit_values(unit, pTB, T, [vB[:, (j // 4) * TT * P + q * P + half * HD:
                                              (j // 4) * TT * P + q * P + (half + 1) * HD] for q in range(b + 1)])

            after(pe, h_roped, "qB7")
            attention(UNITS_B, scoreB, turnB, valuesB)
            project("outB", 4, g_lo.sem, g_lo.value[("dsa", 7)])
            ffn(2)

            norm_total(5)
            J = first_job["mixC"]
            role_done = (c_done, z_done, y_done)
            with pe.Fori(0, 2) as i:
                for q in range(12):
                    pe.wait_ge(role_done[(q - 4) % 3], i * 4 + ((q - 4) // 3 + 3))
                    take(J + q, i, 12)
                    ready = (lambda k: pe.wait_ge(h_lo_done, 5 * KC + k + 1)) if q == 0 else None
                    product(ready, bank(q % 4), [(weights(J + q, k), moving(k)) for k in range(KC)], True, True)\
                        .then_inc(job_done, 1)
            project("outC", 6, y_lo_done, KC + 2, y_hi, y_lo)
            ffn(3)

        @block.scalar
        def _(act):
            def split(first, i, step):
                slot = first % RING
                act.wait_ge(w_in[slot], i * (16 * step // RING) + 16 * (first // RING + 1))
                act.wait_ge(job_done, i * step + (first + 1))
                act.activation(chunk(w_hi, slot, WT), chunk(w_raw, slot, WT), ACT.Copy).then_inc(w_hi_done, 1)

            def lead(first, i=0, step=4):
                if first + LEAD < JOBS or step > 4:
                    split(first + LEAD, i, step)

            def square_x(r, j, parity):
                act.wait_ge(x_done, j + (8 * r + 1))
                if not (r == 0 and isinstance(j, int) and j == 0):
                    act.wait_ge(ss_done, j + 9 * r)
                act.activation(chunk(tmp, parity), x[:, bass.ds(j * T, T)], ACT.Square).then_inc(sq_done, 1)

            def norm(n, shift):
                act.wait_ge(total_done, n + 1)
                act.activation(chunk(tmp, 2), bank(6), ACT.Sqrt, bias=tiny[:, 0:1], scale=1.0 / D)\
                    .then_inc(std_done, 1)
                for k in range(KC):
                    act.wait_ge(normed, KC * n + k + 1)
                    act.activation(chunk(h_hi, k), chunk(tmp, k % 3), ACT.Identity, bias=shift[:, k:k + 1])\
                        .then_inc(h_hi_done, 1)

            def ffn(n, shift):
                norm({0: 0, 1: 2, 2: 4, 3: 6}[n], shift)
                J = first_job[f"ffn{n}"]

                def up(i):
                    for s in range(4):
                        lead(J + s, i)
                        u = s // 2
                        F = n * FC + u
                        if s % 2 == 0:
                            act.wait_ge(job_done, i * 4 + (J + s + 1 + RING))
                            act.wait_ge(hid_done, i * 2 + (F + 1))
                            act.activation(chunk(tmp, u), bank(s), ACT.Silu).then_inc(silu_done, 1)
                        else:
                            act.wait_ge(hid_done, i * 2 + (F + 3))
                            act.activation(hid_hi[:, bass.ds(i * (2 * T) + u * T, T)], chunk(tmp, 2 + u), ACT.Copy)\
                                .then_inc(hid_hi_done, 1)

                def down(i, last):
                    for s in range(8):
                        if not (last and s >= 8 - LEAD):
                            split(J + UP_JOBS + s + LEAD, i, 8)
                        if s % 4 == 3 and n < 3:
                            square_x(2 * n + 1, i * 2 + s // 4, s // 4)

                with act.Fori(0, FC // 2) as i:
                    up(i)
                if n < 3:
                    with act.Fori(0, KC // 2) as i:
                        down(i, False)
                else:
                    with act.Fori(0, KC // 2 - 1) as i:
                        down(i, False)
                    down(KC // 2 - 1, True)

            def project(stage, r):
                J = first_job[stage]
                with act.Fori(0, KC // 4) as i:
                    for s in range(4):
                        lead(J + s, i)
                        square_x(r, i * 4 + s, s % 2)

            def tables(which, rop, sin, cos):
                after(act, d_misc, (which, "clamp"))
                act.activation(sin[:, :], rop[:, 0:T], ACT.Sin).then_inc(a_misc.at((which, "sin")), 1)
                act.activation(rop[:, T:2 * T], rop[:, 0:T], ACT.Abs).then_inc(a_misc.at((which, "abs")), 1)
                after(act, a_misc, (which, "abs"))
                act.activation(cos[:, :], rop[:, T:2 * T], ACT.Sin, bias=tiny[:, 1:2], scale=-1.0)\
                    .then_inc(a_misc.at((which, "cos")), 1)

            def head_square(t, js, hs, src=None):
                n = h_sq.value[t] - 1
                if src is None:
                    act.wait_ge(job_done, js + 1 + RING)
                W = M if t[:2] == "mk" else T
                after_nth(act, h_sum, n - 2)
                act.activation(hs[:, (n % 2) * T:(n % 2) * T + W], bank(js % 4)[:, 0:W] if src is None else src,
                               ACT.Square).then_inc(h_sq.at(t), 1)

            def head_std(t, hr):
                n = h_sq.value[t] - 1
                after(act, h_sum, t)
                if n:
                    after(act, h_normed, h_sq.keys[n - 1])
                W = M if t[:2] == "mk" else T
                act.activation(hr[:, 0:W], bank(4)[:, 0:W], ACT.Sqrt, bias=tiny[:, 0:1], scale=1.0 / HD)\
                    .then_inc(h_std.at(t), 1)

            def exp_unit(unit, sm, p, width, n):
                U = UNITS.index(unit)
                after(act, u_negmax, unit)
                after_nth(act, u_turned, U - 3)
                s = U % 4
                act.activation(p[:, (U % 3) * width:(U % 3) * width + n], sm[:, (U % 2) * width:(U % 2) * width + n],
                               ACT.Exp, bias=small[:, 4 + s:5 + s], scale=SCALE, accum_out=small[:, 8 + s:9 + s])\
                    .then_inc(u_exp.at(unit), 1)

            def keep_turned(unit, pT, width, n):
                U = UNITS.index(unit)
                after(act, u_turned, unit)
                after_nth(act, u_out, U - 2)
                act.activation(pT[:, (U % 2) * width:(U % 2) * width + n], bank(2 + U % 2)[:, 0:n], ACT.Copy)\
                    .then_inc(u_pt.at(unit), 1)

            def group_high(kind, j, dest):
                G = GROUPS.index((kind, j))
                after(act, u_out, (kind, j, TT - 1, 1))
                act.activation(chunk(h_hi, dest), bank(4 + G % 2), ACT.Copy).then_inc(g_hi.at((kind, j)), 1)

            def attention(units, sm, p, width, pT, pT_width, size, dest):
                for u in range(len(units) + 4):
                    if u < len(units):
                        kind, j, b, half = units[u]
                        exp_unit(units[u], sm, p, width, size(units[u]) + (1 if kind == "win" else 0))
                    if 2 <= u < len(units) + 2:
                        keep_turned(units[u - 2], pT, pT_width, size(units[u - 2]))
                    if u >= 4 and units[u - 4][2:] == (TT - 1, 1):
                        kind, j = units[u - 4][:2]
                        group_high(kind, j, dest(kind, j))

            act.wait_ge(consts_in, 16)
            act.activation(c_act[:, :], col("c", 0, KC), ACT.Silu).then_inc(prep, 1)
            act.activation(sink8[:, :], col("sinks", 0, 8), ACT.Copy, scale=1.0 / SCALE).then_inc(a_misc.at("sink8"), 1)
            act.wait_ge(x_in, 16 * KC)
            for j in range(KC):
                square_x(0, j, j % 2)
            for j in range(LEAD):
                act.wait_ge(w_in[j], 16)
                act.activation(chunk(w_hi, j, WT), chunk(w_raw, j, WT), ACT.Copy).then_inc(w_hi_done, 1)
            none = flat[:, 0:KC]
            ffn(0, none)

            norm(1, none)
            act.wait_ge(stage_in, 48)
            tables("tabA", ropA, sinA, cosA)
            act.activation(qA[:, :], memx[:, :], ACT.Square).then_inc(a_misc.at("mem_sq"), 1)
            J = first_job["mixA"]
            for m in range(len(TILES_A) + 2):
                if m < len(TILES_A):
                    t = TILES_A[m]
                    lead(J + m)
                    if has_norm(t):
                        head_square(t, J + m, hsA)
                    elif t[:2] in ("vA", "mv"):
                        act.wait_ge(job_done, J + m + 1 + RING)
                        W = T if t == "vA" else M
                        dest = vA[:, :] if t == "vA" else chunk(mv, int(t[2]), M)
                        act.activation(dest, bank(m % 4)[:, 0:W], ACT.Copy).then_inc(evac.at(t), 1)
                    elif t[0] == "g":
                        act.wait_ge(job_done, J + m + 1 + RING)
                        if t == "g1":
                            after(act, glu_done, "a0")
                        act.activation(sig[:, :], bank(m % 4), ACT.Sigmoid).then_inc(evac.at(t), 1)
                if 1 <= m and m - 1 < len(TILES_A) and has_norm(TILES_A[m - 1]):
                    head_std(TILES_A[m - 1], hrA)
                if m == 5:
                    after(act, p_misc, "mem_total")
                    act.activation(ssum[:, M:2 * M], bank(6)[:, 0:M], ACT.Sqrt, bias=tiny[:, 0:1], scale=1.0 / D)\
                        .then_inc(a_misc.at("mem_std"), 1)
                if m == 7:
                    after(act, d_misc, ("mem", KC - 1))
                    act.activation(mh_hi[:, :], memx[:, :], ACT.Copy).then_inc(a_misc.at("mem_hi"), 1)
            for c in range(2):
                after(act, d_misc, f"ctr{c}")
                act.activation(chunk(hsA, c), chunk(conv, c), ACT.Square).then_inc(a_misc.at(f"conv_sq{c}"), 1)
            after(act, p_misc, "conv_var")
            act.activation(hrA[:, :], bank(7), ACT.Sqrt, bias=tiny[:, 0:1], scale=1.0 / (2 * P))\
                .then_inc(a_misc.at("conv_std"), 1)
            for c in range(2):
                after(act, d_misc, f"conv_n{c}")
                act.activation(chunk(conv, c), chunk(conv, c), ACT.Silu, bias=col("cln_b", c))\
                    .then_inc(a_misc.at(f"conv_y{c}"), 1)
            act.wait_ge(job_done, J + len(TILES_A) + RING)
            for c in range(2):
                after(act, a_misc, f"conv_y{c}")
                act.activation(chunk(h_hi, 4 + c), chunk(conv, c), ACT.Copy).then_inc(g_hi.at(f"c{c}"), 1)
            attention(UNITS_A, smA, pA, M + 8, pTA, M,
                      lambda u: P if u[0] == "win" and u[2] == 0 else 2 * P,
                      lambda kind, j: j if kind == "win" else 6 + j)
            project("outA", 2)
            ffn(1, none)

            norm(3, modc[:, 0:KC])
            act.wait_ge(stage_in, 80)
            tables("tabB", ropB, sinB, cosB)
            J = first_job["mixB"]
            for m in range(len(TILES_B) + 2):
                if m < len(TILES_B):
                    t = TILES_B[m]
                    lead(J + m)
                    if t == "ki":
                        act.wait_ge(job_done, J + m + 1 + RING)
                        act.activation(kraw[:, :], bank(m % 4), ACT.Copy).then_inc(evac.at(t), 1)
                    elif t == "wi":
                        act.wait_ge(job_done, J + m + 1 + RING)
                        act.activation(wi[:, :], bank(m % 4)[:, 0:TT * 8], ACT.Copy, scale=WI_SCALE)\
                            .then_inc(evac.at(t), 1)
                    elif t[:2] == "vB":
                        act.wait_ge(job_done, J + m + 1 + RING)
                        act.activation(chunk(vB, int(t[2])), bank(m % 4), ACT.Copy).then_inc(evac.at(t), 1)
                    elif has_norm(t):
                        head_square(t, J + m, hsB)
                if m == 1:
                    after(act, d_misc, "ki_ctr")
                    head_square("ki", J, hsB, src=kraw[:, :])
                if m == 2:
                    head_std("ki", hrB)
                if 2 <= m <= len(TILES_B) and has_norm(TILES_B[m - 1]):
                    head_std(TILES_B[m - 1], hrB)
                if 8 <= m <= 10:
                    b = m - 7
                    n = (b + 1) * P
                    for h in range(8):
                        I = IDX.index((b, h))
                        after(act, i_score, (b, h))
                        after_nth(act, i_sum, I - 2)
                        act.activation(relu[:, (I % 2) * T:(I % 2) * T + n], bank(6 + I % 2)[:, 0:n], ACT.Relu)\
                            .then_inc(i_relu.at((b, h)), 1)
            attention(UNITS_B, smB, pB, T, pTB, T, lambda u: (u[2] + 1) * P, lambda kind, j: j)
            project("outB", 4)
            ffn(2, modc[:, 3 * KC:4 * KC])

            norm(5, modc[:, 6 * KC:7 * KC])
            J = first_job["mixC"]
            with act.Fori(0, 2) as i:
                for q in range(12):
                    lead(J + q, i, 12)
                    l, role = q // 3, q % 3
                    if role == 0:
                        act.wait_ge(job_done, i * 12 + (J + q + 1 + RING))
                        act.wait_ge(z_done, i * 4 + (l + 1))
                        act.activation(chunk(c_sb, l % 2), bank(q % 4), ACT.Copy).then_inc(c_done, 1)
                    if role == 2:
                        act.wait_ge(y_done, i * 4 + (l + 3))
                        act.activation(y_hi[:, bass.ds(i * (4 * T) + l * T, T)], chunk(tap, l % 2), ACT.Copy).then_inc(y_hi_done, 1)
            project("outC", 6)
            ffn(3, modc[:, 9 * KC:10 * KC])

        @block.vector
        def _(dve):
            def split(first, i=0, step=4):
                slot = first % RING
                dve.wait_ge(w_hi_done, i * step + (first + 1))
                dve.tensor_tensor(chunk(w_lo, slot, WT), chunk(w_raw, slot, WT), f32(chunk(w_hi, slot, WT)),
                                  ALU.subtract).then_inc(w_lo_done, 1)

            def lead(first, i=0, step=4):
                if first + LEAD < JOBS or step > 4:
                    split(first + LEAD, i, step)

            def sum_x(r, j, parity):
                dve.wait_ge(sq_done, j + (8 * r + 1))
                dve.wait_ge(ss_done, j + (9 * r + 1))
                dve.tensor_tensor(ssum[:, :], ssum[:, :], chunk(tmp, parity), ALU.add).then_inc(ss_done, 1)

            def clear_sum(r):
                if r:
                    dve.wait_ge(total_done, r)
                dve.memset(ssum[:, :], 0.0).then_inc(ss_done, 1)

            def update_x(r, j, b, gates, job, i, step):
                dve.wait_ge(job_done, i * step + (job + 1 + RING))
                here = x[:, bass.ds(j * T, T)]
                dve.scalar_tensor_tensor(here, bank(b), gates[:, bass.ds(j, 1)], here, ALU.mult, ALU.add)\
                    .then_inc(x_done, 1)

            def norm(n, gain, shift):
                rstd = chunk(tmp, 3)
                dve.wait_ge(std_done, n + 1)
                dve.reciprocal(rstd, chunk(tmp, 2)).then_inc(rstd_done, 1)
                dve.wait_ge(rstd_done, n + 1)
                for k in range(KC + 1):
                    if k < KC:
                        if k > 2:
                            dve.wait_ge(h_lo_done, KC * n + k - 2)
                        dve.scalar_tensor_tensor(chunk(tmp, k % 3), chunk(x, k), gain[:, k:k + 1], rstd,
                                                 ALU.mult, ALU.mult).then_inc(normed, 1)
                    if k:
                        dve.wait_ge(h_hi_done, KC * n + k)
                        dve.scalar_tensor_tensor(chunk(h_lo, k - 1), chunk(tmp, (k - 1) % 3), shift[:, k - 1:k],
                                                 f32(chunk(h_hi, k - 1)), ALU.add, ALU.subtract)\
                            .then_inc(h_lo_done, 1)

            def ffn(n, gain, shift, gates):
                norm({0: 0, 1: 2, 2: 4, 3: 6}[n], gain, shift)
                J = first_job[f"ffn{n}"]

                def modulate(a, k):
                    piece = k // 2
                    w = ada_raw[:, (piece % 2) * 2 * ADA + (k % 2) * ADA:(piece % 2) * 2 * ADA + (k % 2 + 1) * ADA]
                    dve.wait_ge(ada_in[piece % 2], a * 32 + 16 * (piece // 2 + 1))
                    if k == 0:
                        dve.wait_ge(ada_mm_done, a + 1)
                        dve.tensor_scalar(ada_sum[:, :], w, c_act[:, 0:1], None, ALU.mult).then_inc(ada_sum_done, 1)
                    else:
                        dve.wait_ge(ada_sum_done, a * 8 + (k + 4))
                        dve.scalar_tensor_tensor(ada_sum[:, :], w, c_act[:, k:k + 1], ada_sum[:, :],
                                                 ALU.mult, ALU.add).then_inc(ada_sum_done, 1)

                def hidden_low(i, u):
                    dve.wait_ge(hid_hi_done, i * 2 + (n * FC + u + 1))
                    at = bass.ds(i * (2 * T) + u * T, T)
                    dve.tensor_tensor(hid_lo[:, at], chunk(tmp, 2 + u), f32(hid_hi[:, at]), ALU.subtract)\
                        .then_inc(hid_lo_done, 1)

                def up(i, modulation):
                    for s in range(4):
                        lead(J + s, i)
                        u = s // 2
                        if modulation:
                            for k in range(2 * s, 2 * s + 2):
                                modulate(i + n * ADA_PER_FFN, k)
                        if s % 2:
                            dve.wait_ge(job_done, i * 4 + (J + s + 1 + RING))
                            dve.wait_ge(silu_done, i * 2 + (n * FC + u + 1))
                            dve.wait_ge(hid_lo_done, i * 2 + (n * FC + u + 1))
                            dve.tensor_tensor(chunk(tmp, 2 + u), chunk(tmp, u), bank(s), ALU.mult)\
                                .then_inc(hid_done, 1)
                            hidden_low(i, u)
                    if modulation:
                        a = i + n * ADA_PER_FFN
                        dve.wait_ge(ada_mm_done, a + 2)
                        dve.tensor_tensor(modc[:, bass.ds(a * 4, 4)], bank(7)[:, 0:4],
                                          cols[:, bass.ds(a * 4 + COLS["ada_b"][0], 4)], ALU.add)\
                            .then_inc(ada_done, 1)

                def down(i, last):
                    for s in range(8):
                        if not (last and s >= 8 - LEAD):
                            split(J + UP_JOBS + s + LEAD, i, 8)
                        if s % 4 == 3:
                            t = s // 4
                            update_x(2 * n + 1, i * 2 + t, 4 + t, gates, J + UP_JOBS + s, i, 8)
                            if n < 3:
                                sum_x(2 * n + 1, i * 2 + t, t)

                if n < 3:
                    with dve.Fori(0, ADA_PER_FFN) as i:
                        up(i, True)
                with dve.Fori(ADA_PER_FFN if n < 3 else 0, FC // 2) as i:
                    up(i, False)
                if n < 3:
                    clear_sum(2 * n + 1)
                    with dve.Fori(0, KC // 2) as i:
                        down(i, False)
                else:
                    with dve.Fori(0, KC // 2 - 1) as i:
                        down(i, False)
                    down(KC // 2 - 1, True)

            def project(stage, r, gates):
                J = first_job[stage]
                clear_sum(r)
                with dve.Fori(0, KC // 4) as i:
                    for s in range(4):
                        lead(J + s, i)
                        update_x(r, i * 4 + s, s, gates, J + s, i, 4)
                        sum_x(r, i * 4 + s, s % 2)

            def tables(which, rop, freq):
                one, two = chunk(rop, 0), chunk(rop, 1)

                def did(step):
                    return d_misc.at((which, step))

                def stands(step):
                    after(dve, d_misc, (which, step))

                dve.tensor_copy(two, one.bitcast(I32)).then_inc(did("pos"), 1)
                stands("pos")
                dve.tensor_scalar(one, two, freq, None, ALU.mult).then_inc(did("ang"), 1)
                stands("ang")
                dve.tensor_scalar(two, one, 1.0 / TWO_PI, ROUNDER, ALU.mult, ALU.add).then_inc(did("turns"), 1)
                stands("turns")
                dve.tensor_scalar(two, two, ROUNDER, None, ALU.subtract).then_inc(did("whole"), 1)
                for part, step, before in ((PI_A, "r1", "whole"), (PI_B, "r2", "r1"), (PI_C, "r3", "r2")):
                    stands(before)
                    dve.scalar_tensor_tensor(one, two, -part, one, ALU.mult, ALU.add).then_inc(did(step), 1)
                stands("r3")
                dve.tensor_scalar(one, one, PI_CLAMP, -PI_CLAMP, ALU.min, ALU.max).then_inc(did("clamp"), 1)

            def head_norm(t, js, gain, hr, dest, src=None, bias=None):
                W = M if t[:2] == "mk" else T
                after(dve, h_std, t)
                dve.reciprocal(hr[:, 0:W], hr[:, 0:W]).then_inc(h_rstd.at(t), 1)
                after(dve, h_rstd, t)
                if has_rope(t):
                    after_nth(dve, h_sin, h_rot.value[t] - 3)
                if bias is None:
                    dve.scalar_tensor_tensor(dest, bank(js % 4)[:, 0:W], gain, hr[:, 0:W], ALU.mult, ALU.mult)\
                        .then_inc(h_normed.at(t), 1)
                else:
                    dve.scalar_tensor_tensor(dest, src, gain, hr[:, 0:W], ALU.mult, ALU.mult)\
                        .then_inc(d_misc.at("ki_g"), 1)
                    after(dve, d_misc, "ki_g")
                    dve.tensor_scalar(dest, dest, bias, None, ALU.add).then_inc(h_normed.at(t), 1)

            def head_rope(t, qn, rop, sin, cos, dest):
                n = h_rot.value[t] - 1
                after(dve, h_normed, t)
                after_nth(dve, h_roped, n - 1)
                dve.tensor_tensor(chunk(rop, 0), chunk(qn, n % 2), cos[:, :], ALU.mult)
                after(dve, h_rot, t)
                dve.tensor_tensor(chunk(rop, 1), bank(5), sin[:, :], ALU.mult).then_inc(h_sin.at(t), 1)
                after(dve, h_sin, t)
                dve.tensor_tensor(dest, chunk(rop, 0), chunk(rop, 1), ALU.add).then_inc(h_roped.at(t), 1)

            def turned_of(t, qn):
                return chunk(qn, (h_rot.value[t] - 1) % 2)

            def mask_unit(unit, sm, width, mask, n, sink):
                U = UNITS.index(unit)
                s, at = U % 4, (U % 2) * width
                after(dve, u_score, unit)
                after_nth(dve, u_exp, U - 2)
                if sink is not None:
                    dve.tensor_copy(sm[:, at + n:at + n + 1], sink)
                dve.tensor_tensor_reduce(sm[:, at:at + n], bank(U % 2)[:, 0:n], mask, 1.0, NO_SINK, ALU.add, ALU.max,
                                         small[:, s:s + 1]).then_inc(u_masked.at(unit), 1)
                after(dve, u_masked, unit)
                if sink is not None:
                    dve.tensor_scalar(small[:, 4 + s:5 + s], small[:, s:s + 1], sink, -SCALE, ALU.max, ALU.mult)\
                        .then_inc(u_negmax.at(unit), 1)
                else:
                    dve.tensor_scalar(small[:, 4 + s:5 + s], small[:, s:s + 1], -SCALE, None, ALU.mult)\
                        .then_inc(u_negmax.at(unit), 1)

            def weigh_unit(unit, p, width, n):
                U = UNITS.index(unit)
                s, at = U % 4, (U % 3) * width
                after(dve, u_exp, unit)
                dve.reciprocal(small[:, 12 + s:13 + s], small[:, 8 + s:9 + s]).then_inc(u_inv.at(unit), 1)
                after(dve, u_inv, unit)
                dve.tensor_scalar(p[:, at:at + n], p[:, at:at + n], small[:, 12 + s:13 + s], None, ALU.mult)\
                    .then_inc(u_prob.at(unit), 1)

            def group_low(kind, j, dest):
                G = GROUPS.index((kind, j))
                after(dve, g_hi, (kind, j))
                dve.tensor_tensor(chunk(h_lo, dest), bank(4 + G % 2), f32(chunk(h_hi, dest)), ALU.subtract)\
                    .then_inc(g_lo.at((kind, j)), 1)

            def attention(units, mask, weigh, dest):
                for u in range(len(units) + 5):
                    if u < len(units):
                        mask(units[u])
                    if 1 <= u < len(units) + 1:
                        weigh(units[u - 1])
                    if u >= 5 and units[u - 5][2:] == (TT - 1, 1):
                        kind, j = units[u - 5][:2]
                        group_low(kind, j, dest(kind, j))

            dve.memset(ones[:, :], 1.0).then_inc(job_done, RING)
            dve.memset(tiny[:, 0:1], EPS).then_inc(w_lo_done, RING)
            dve.memset(tiny[:, 1:2], math.pi / 2).then_inc(hid_done, 2)
            dve.memset(top8[:, 5:6], 0.0).then_inc(hid_lo_done, 2)
            dve.memset(top8[:, 6:7], 0.0).then_inc(tap_done, 4)
            dve.memset(top8[:, 7:8], 0.0).then_inc(y_lo_done, 2)
            dve.memset(flat[:, 0:KC], 0.0).then_inc(ada_sum_done, 4)
            dve.memset(flat[:, KC:2 * KC], 0.5).then_inc(ada_mm_done, 1)
            dve.memset(flat[:, 2 * KC:3 * KC], 1.0).then_inc(ada_done, 1)
            dve.memset(top8[:, 0:1], 0.0).then_inc(x_done, KC)
            dve.memset(top8[:, 1:2], 0.0).then_inc(c_done, 2)
            dve.memset(top8[:, 2:3], 0.0).then_inc(z_done, 2)
            dve.memset(top8[:, 3:4], 0.0).then_inc(y_done, 2)
            none, half, whole = (flat[:, n * KC:(n + 1) * KC] for n in range(3))
            clear_sum(0)
            for j in range(KC):
                sum_x(0, j, j % 2)
            for j in range(LEAD):
                split(j)
            dve.wait_ge(prep, 1)
            ffn(0, col("g_ffn1", 0, KC), none, half)

            norm(1, col("g_mix", 0, KC), none)
            dve.wait_ge(stage_in, 48)
            tables("tabA", ropA, col("freq_a"))
            dve.memset(glu[:, 0:PAD_A], 0.0)
            dve.memset(glu[:, PAD_A + T:2 * PAD_A + T], 0.0)
            dve.memset(zeroA[:, :], 0.0)
            after(dve, a_misc, ("tabA", "cos"))
            J = first_job["mixA"]
            GAINS = {"kA": "g_k", "qA": "g_q", "mq": "g_mq", "mk": "g_mk"}
            taps = [(t, c) for t in range(CONV_A) for c in range(2)]

            def conv_tap(t, c):
                src = glu[:, c * (PAD_A + T) + t:c * (PAD_A + T) + t + T]
                w = col("w_dw", c * CONV_A + t)
                if t == 0:
                    dve.tensor_scalar(chunk(conv, c), src, w, col("b_dw", c), ALU.mult, ALU.add)\
                        .then_inc(d_misc.at(("conv", t, c)), 1)
                else:
                    after(dve, d_misc, ("conv", t - 1, c))
                    dve.scalar_tensor_tensor(chunk(conv, c), src, w, chunk(conv, c), ALU.mult, ALU.add)\
                        .then_inc(d_misc.at(("conv", t, c)), 1)

            for m in range(len(TILES_A) + 2):
                if m < len(TILES_A):
                    t = TILES_A[m]
                    lead(J + m)
                    if t[0] == "a":
                        c = int(t[1])
                        after(dve, evac, f"g{c}")
                        dve.wait_ge(job_done, J + m + 1 + RING)
                        dve.tensor_tensor(glu[:, c * (PAD_A + T) + PAD_A:(c + 1) * (PAD_A + T)], sig[:, :], bank(m % 4),
                                          ALU.mult).then_inc(glu_done.at(t), 1)
                if m >= 1 and m - 1 < len(TILES_A) and has_norm(TILES_A[m - 1]):
                    t = TILES_A[m - 1]
                    dest = {"mq": lambda: chunk(mq, int(t[2])), "mk": lambda: chunk(mk, int(t[2]), M)}.get(
                        t[:2], lambda: turned_of(t, qnA))()
                    head_norm(t, J + m - 1, col(GAINS[t[:2]]), hrA, dest)
                if m >= 2 and has_rope(TILES_A[m - 2]):
                    t = TILES_A[m - 2]
                    head_rope(t, qnA, ropA, sinA, cosA, kA[:, :] if t == "kA" else chunk(qA, int(t[2])))
                if m == 1:
                    after(dve, a_misc, "mem_sq")
                    dve.tensor_reduce(ssum[:, 0:M], qA[:, :].rearrange("p (k t) -> p t k", k=KC), AX_X, ALU.add)\
                        .then_inc(d_misc.at("mem_sum"), 1)
                if m == 6:
                    after(dve, a_misc, "mem_std")
                    dve.reciprocal(ssum[:, M:2 * M], ssum[:, M:2 * M]).then_inc(d_misc.at("mem_rstd"), 1)
                    after(dve, d_misc, "mem_rstd")
                    for k in range(KC):
                        dve.scalar_tensor_tensor(chunk(memx, k, M), chunk(memx, k, M), col("g_mem", k), ssum[:, M:2 * M],
                                                 ALU.mult, ALU.mult).then_inc(d_misc.at(("mem", k)), 1)
                if m == 8:
                    after(dve, a_misc, "mem_hi")
                    dve.tensor_tensor(mh_lo[:, :], memx[:, :], f32(mh_hi[:, :]), ALU.subtract)\
                        .then_inc(d_misc.at("mem_lo"), 1)
                if m == 10:
                    after(dve, glu_done, "a1")
                if m >= 10:
                    for t, c in taps[(m - 10) * 8:(m - 9) * 8]:
                        conv_tap(t, c)
            after(dve, p_misc, "conv_total")
            for c in range(2):
                dve.scalar_tensor_tensor(chunk(conv, c), bank(6), -1.0 / (2 * P), chunk(conv, c), ALU.mult, ALU.add)\
                    .then_inc(d_misc.at(f"ctr{c}"), 1)
            after(dve, a_misc, "conv_std")
            dve.reciprocal(hrA[:, :], hrA[:, :]).then_inc(d_misc.at("conv_rstd"), 1)
            after(dve, d_misc, "conv_rstd")
            for c in range(2):
                dve.scalar_tensor_tensor(chunk(conv, c), chunk(conv, c), col("cln_g", c), hrA[:, :], ALU.mult, ALU.mult)\
                    .then_inc(d_misc.at(f"conv_n{c}"), 1)
            for c in range(2):
                after(dve, g_hi, f"c{c}")
                dve.tensor_tensor(chunk(h_lo, 4 + c), chunk(conv, c), f32(chunk(h_hi, 4 + c)), ALU.subtract)\
                    .then_inc(g_lo.at(f"c{c}"), 1)

            def maskA(unit):
                kind, j, b, half_ = unit
                if kind == "win":
                    lo, n = (P, P) if b == 0 else (0, 2 * P)
                    at = MATS["mask"][0] + lo
                    mask_unit(unit, smA, M + 8, matsA[:, at:at + n], n, sink8[:, j + 4 * half_:j + 4 * half_ + 1])
                else:
                    mask_unit(unit, smA, M + 8, zeroA[:, :], M, None)

            after(dve, a_misc, "sink8")
            attention(UNITS_A, maskA,
                      lambda u: weigh_unit(u, pA, M + 8, P if u[0] == "win" and u[2] == 0 else 2 * P),
                      lambda kind, j: j if kind == "win" else 6 + j)
            project("outA", 2, whole)
            ffn(1, col("g_ffn2", 0, KC), none, half)

            def gains(n, g, scale_at, need):
                dve.wait_ge(ada_done, need + 1)
                dve.scalar_tensor_tensor(geff[:, n * KC:(n + 1) * KC], modc[:, scale_at * KC:(scale_at + 1) * KC], 1.0,
                                         col(g, 0, KC), ALU.add, ALU.mult).then_inc(d_misc.at(f"geff{n}"), 1)

            gains(0, "n1_0", 1, 12)
            gains(1, "n2_0", 4, 12)
            after(dve, d_misc, "geff1")
            norm(3, geff[:, 0:KC], modc[:, 0:KC])
            dve.wait_ge(stage_in, 80)
            tables("tabB", ropB, col("freq_b"))
            after(dve, a_misc, ("tabB", "cos"))
            J = first_job["mixB"]
            starts = {1: 0, 2: 2 * P, 3: 5 * P}

            def index_sum(b, h):
                n = (b + 1) * P
                I = IDX.index((b, h))
                s = score[:, starts[b]:starts[b] + n]
                r = relu[:, (I % 2) * T:(I % 2) * T + n]
                w = wi[:, b * 8 + h:b * 8 + h + 1]
                after(dve, i_relu, (b, h))
                if h == 0:
                    dve.tensor_scalar(s, r, w, None, ALU.mult).then_inc(i_sum.at((b, h)), 1)
                else:
                    after(dve, i_sum, (b, h - 1))
                    dve.scalar_tensor_tensor(s, r, w, s, ALU.mult, ALU.add).then_inc(i_sum.at((b, h)), 1)

            def take_top(b, rounds):
                n = (b + 1) * P
                s = score[:, starts[b]:starts[b] + n]
                for r in rounds:
                    if r == 0:
                        after(dve, i_sum, (b, 7))
                        at = MATS["mask"][0] + P
                        dve.tensor_tensor(s[:, n - P:n], s[:, n - P:n], matsB[:, at:at + P], ALU.add)\
                            .then_inc(top.at((b, "tri")), 1)
                    after(dve, top, (b, "tri") if r == 0 else (b, r - 1, "take"))
                    dve.max(top8[:, :], s).then_inc(top.at((b, r, "max")), 1)
                    after(dve, top, (b, r, "max"))
                    dve.match_replace(s, top8[:, :], s, TAKEN).then_inc(top.at((b, r, "take")), 1)
                    if r == ROUNDS - 1:
                        after(dve, top, (b, r, "take"))
                        dve.tensor_scalar(dmask[:, starts[b]:starts[b] + n], s, TAKEN / 2, MASKED, ALU.is_gt, ALU.mult)\
                            .then_inc(top.at((b, "mask")), 1)

            for m in range(len(TILES_B) + 2):
                if m < len(TILES_B):
                    lead(J + m)
                if m == 1:
                    after(dve, p_misc, "ki_total")
                    dve.scalar_tensor_tensor(kraw[:, :], bank(6), -1.0 / HD, kraw[:, :], ALU.mult, ALU.add)\
                        .then_inc(d_misc.at("ki_ctr"), 1)
                if m == 2:
                    head_norm("ki", J, col("ln_g"), hrB, turned_of("ki", qnB), src=kraw[:, :], bias=col("ln_b"))
                if 2 <= m <= len(TILES_B):
                    t = TILES_B[m - 1]
                    if has_norm(t):
                        head_norm(t, J + m - 1, col("g_k2" if t[0] == "k" else "g_q2"), hrB, turned_of(t, qnB))
                    elif has_rope(t):
                        dve.wait_ge(job_done, J + m + RING)
                        after_nth(dve, h_sin, h_rot.value[t] - 3)
                        dve.tensor_copy(turned_of(t, qnB), bank((J + m - 1) % 4)).then_inc(h_normed.at(t), 1)
                if m == 3:
                    head_rope("ki", qnB, ropB, sinB, cosB, ki[:, :])
                if m >= 3 and has_rope(TILES_B[m - 2]):
                    t = TILES_B[m - 2]
                    whole_of = {"kB": kB, "qB": qB, "qi": qi}[t[:2]]
                    head_rope(t, qnB, ropB, sinB, cosB, chunk(whole_of, int(t[2])))
                if 8 <= m <= 10:
                    for h in range(8):
                        index_sum(m - 7, h)
                if m in (9, 10):
                    take_top(1, range((m - 9) * 8, (m - 8) * 8))
                if m in (11, 12, 13):
                    take_top(2, range((m - 11) * 6, min((m - 10) * 6, ROUNDS)))
                if m in (14, 15, 16, 17):
                    take_top(3, range((m - 14) * 4, (m - 13) * 4))

            def maskB(unit):
                _, j, b, half_ = unit
                if b == 0:
                    at = MATS["mask"][0] + P
                    mask_unit(unit, smB, T, matsB[:, at:at + P], P, None)
                else:
                    if j == 0 and half_ == 0:
                        after(dve, top, (b, "mask"))
                    n = (b + 1) * P
                    mask_unit(unit, smB, T, dmask[:, starts[b]:starts[b] + n], n, None)

            attention(UNITS_B, maskB, lambda u: weigh_unit(u, pB, T, (u[2] + 1) * P), lambda kind, j: j)
            project("outB", 4, modc[:, 2 * KC:3 * KC])
            ffn(2, geff[:, KC:2 * KC], modc[:, 3 * KC:4 * KC], modc[:, 5 * KC:6 * KC])

            gains(2, "n1_1", 7, 24)
            gains(3, "n2_1", 10, 24)
            after(dve, d_misc, "geff3")
            norm(5, geff[:, 2 * KC:3 * KC], modc[:, 6 * KC:7 * KC])
            for l in range(2):
                dve.memset(zc[:, l * (PAD_B + T):l * (PAD_B + T) + PAD_B], 0.0)
            J = first_job["mixC"]
            with dve.Fori(0, 2) as i:
                for q in range(12):
                    lead(J + q, i, 12)
                    l, role = q // 3, q % 3
                    z0 = (l % 2) * (PAD_B + T)
                    y = chunk(tap, l % 2)
                    if role == 1:
                        dve.wait_ge(c_done, i * 4 + (l + 3))
                        dve.wait_ge(job_done, i * 12 + (J + q + 1 + RING))
                        dve.wait_ge(tap_done, i * 12 + (3 * l + 1))
                        dve.tensor_tensor(zc[:, z0 + PAD_B:z0 + PAD_B + T], chunk(c_sb, l % 2), bank(q % 4), ALU.mult)\
                            .then_inc(z_done, 1)
                        dve.wait_ge(z_done, i * 4 + (l + 3))
                        for t in range(CONV_B):
                            w = cols[:, bass.ds(i * (4 * CONV_B) + (COLS["conv_w"][0] + l * CONV_B + t), 1)]
                            z = zc[:, z0 + t:z0 + t + T]
                            if t == 0:
                                dve.wait_ge(y_lo_done, i * 4 + (l + 1))
                                dve.tensor_scalar(y, z, w, None, ALU.mult).then_inc(tap_done, 1)
                            else:
                                dve.wait_ge(tap_done, i * 12 + (3 * l + t + 4))
                                dve.scalar_tensor_tensor(y, z, w, y, ALU.mult, ALU.add).then_inc(tap_done, 1)
                    if role == 2:
                        dve.wait_ge(job_done, i * 12 + (J + q + 1 + RING))
                        dve.wait_ge(tap_done, i * 12 + (3 * l + 7))
                        dve.tensor_tensor(y, y, bank(q % 4), ALU.mult).then_inc(y_done, 1)
                        dve.wait_ge(y_hi_done, i * 4 + (l + 1))
                        at = bass.ds(i * (4 * T) + l * T, T)
                        dve.tensor_tensor(y_lo[:, at], y, f32(y_hi[:, at]), ALU.subtract).then_inc(y_lo_done, 1)
            project("outC", 6, modc[:, 8 * KC:9 * KC])
            ffn(3, geff[:, 3 * KC:4 * KC], modc[:, 9 * KC:10 * KC], modc[:, 11 * KC:12 * KC])


def matrices():
    m = np.zeros((P, NMATS), np.float32)
    m[:, 0:P] = np.eye(P)
    f = np.zeros((P, 2), np.float32)
    for p in range(P):
        head, d = p // HD, p % HD
        m[p, P + head * HD:P + (head + 1) * HD] = 1.0
        for which, width, theta, n in ((2, 16, 500000.0, 0), (3, HD, 10000.0, 1)):
            if d < width:
                h = width // 2
                partner = head * HD + (d + h) % width
                m[partner, which * P + p] = -1.0 if d < h else 1.0
                f[p, n] = theta ** (-(d % h) / h)
    q, k = np.arange(P)[:, None], np.arange(2 * P)[None, :]
    rel = q + P - k
    m[:, 4 * P:] = np.where((rel >= 0) & (rel < P), 0.0, MASKED)
    return m, f


def columns(v):
    v = np.asarray(v).reshape(-1, P)
    return v.T


def tiles(w, cols=P):
    w = np.asarray(w)
    return np.ascontiguousarray(w.reshape(w.shape[0] // P, P, -1, cols).transpose(2, 1, 0, 3)).reshape(
        w.shape[1] // cols, P, -1)


def heads_apart(w, axis, order):
    w = np.moveaxis(np.asarray(w), axis, 0)
    w = w.reshape((-1, HD) + w.shape[1:])[order]
    return np.moveaxis(w.reshape((-1,) + w.shape[2:]), 0, axis)


def layout(v):
    a = {}
    mats, freq = matrices()
    a["mats"] = mats
    g = {k: np.asarray(t) for k, t in v.items()}
    twice = lambda t: np.concatenate([t, t]).reshape(P, 1)
    parts = {
        "g_ffn1": columns(g["g_ffn1"]), "g_mix": columns(g["g_mix"]), "g_ffn2": columns(g["g_ffn2"]),
        "n1_0": columns(g["norm1_g_2"][0]), "n2_0": columns(g["norm2_g_2"][0]), "n1_1": columns(g["norm1_g_2"][1]),
        "n2_1": columns(g["norm2_g_2"][1]), "g_mem": columns(g["g_mem"]), "g_q": twice(g["g_q"][0]),
        "g_k": twice(g["g_k"][0]), "g_mq": twice(g["g_mq"][0]), "g_mk": twice(g["g_mk"][0]),
        "g_q2": twice(g["attn_q_norm_g_2"][0]), "g_k2": twice(g["attn_k_norm_g_2"][0]),
        "ln_g": twice(g["idx_k_ln_g_2"][0]), "ln_b": twice(g["idx_k_ln_b_2"][0]), "b_dw": columns(g["b_dw"]),
        "cln_g": columns(g["g_conv_ln"]), "cln_b": columns(g["b_conv_ln"]),
        "w_dw": g["w_dw"][0].reshape(CONV_A, 2, P).transpose(2, 1, 0).reshape(P, -1),
        "sinks": np.broadcast_to(g["sinks"].reshape(1, 8), (P, 8)),
        "conv_w": g["conv_w_2"][0].reshape(CONV_B, KC, P).transpose(2, 1, 0).reshape(P, -1),
        "c": columns(g["c_2"]), "ada_b": columns(g["ada_b_2"]), "freq_a": freq[:, 0:1], "freq_b": freq[:, 1:2],
    }
    a["cols"] = np.ascontiguousarray(np.concatenate([parts[k] for k in COLS], axis=1))
    a["x"] = np.ascontiguousarray(g["x"][0].T).reshape(KC, P, T)
    a["mem"] = np.ascontiguousarray(g["mem"][0].T.reshape(KC, P, M).transpose(1, 0, 2)).reshape(P, KC * M)
    a["positions"] = np.ascontiguousarray(np.broadcast_to(g["positions"].reshape(1, T), (P, T)))
    a["positions_2"] = np.ascontiguousarray(np.broadcast_to(g["positions_2"].reshape(1, T), (P, T)))
    ffns = [("w_ffn1_gate", "w_ffn1_up", "w_ffn1_down", 0), ("w_ffn2_gate", "w_ffn2_up", "w_ffn2_down", 0),
            ("ffn_w_gate_2", "ffn_w_up_2", "ffn_w_down_2", 0), ("ffn_w_gate_2", "ffn_w_up_2", "ffn_w_down_2", 1)]
    for n, (gate, up, down, l) in enumerate(ffns):
        a[f"gate{n}"], a[f"up{n}"], a[f"down{n}"] = tiles(g[gate][l]), tiles(g[up][l]), tiles(g[down][l])
    w = g["w_in"][0]
    q, k, vv, u, mq = np.split(w, [512, 640, 768, 1280], axis=1)
    order = [h for j in range(4) for h in (j, j + 4)]
    ua, ug = u[:, 0:2 * P], u[:, 2 * P:]
    q = heads_apart(q, 1, order)
    w = np.concatenate([vv, k, q, ug[:, :P], ua[:, :P], ug[:, P:], ua[:, P:], mq, g["w_mem_kv"][0]], axis=1)
    a["w_mix"] = tiles(w)
    w = g["w_out"][0]
    a["w_out"] = tiles(np.concatenate([heads_apart(w[:512], 0, order), w[512:]], axis=0))
    w = g["attn_w_in_2"][0]
    q, k, vv, qi, ki, wi = np.split(w, [1024, 1280, 1536, 2048, 2112], axis=1)
    order = [h for pair in range(2) for r in range(4) for h in (8 * pair + r, 8 * pair + 4 + r)]
    q = heads_apart(q, 1, order)
    main = tiles(np.concatenate([ki, ki, qi, vv, k, q], axis=1))
    wt = np.zeros((1, P, WT), np.float32)
    wt[:, :, :KC * 8] = tiles(wi, 8)
    a["w_mix_b"] = np.concatenate([main[0:1], wt, main[1:]], axis=0)
    a["w_out_b"] = tiles(heads_apart(g["attn_w_out_2"][0], 0, order))
    b_gate, c_gate, uu = (tiles(t) for t in np.split(g["conv_w_in_2"][0], 3, axis=1))
    a["w_mix_c"] = np.ascontiguousarray(np.stack([c_gate, uu, b_gate], axis=1)).reshape(3 * KC, P, WT)
    a["w_out_c"] = tiles(g["conv_w_out_2"][0])
    a["ada_w"] = np.concatenate([tiles(g["ada_w_2"][l], ADA) for l in range(2)], axis=0)
    return a


def kernel(**inputs):
    import concourse.bacc as bacc
    from concourse.bass_utils import run_bass_kernel_spmd

    arrays = layout(inputs)
    nc = bacc.Bacc("TRN2", target_bir_lowering=False, num_devices=1)
    aps = {n: nc.dram_tensor(f"in_{n}", a.shape, mybir.dt.from_np(a.dtype), kind="ExternalInput").ap()
           for n, a in arrays.items()}
    out = nc.dram_tensor("out", (KC, P, T), F32, kind="ExternalOutput").ap()
    build(nc, aps, out)
    result = run_bass_kernel_spmd(nc, [{f"in_{n}": a for n, a in arrays.items()}], core_ids=[0])
    got = result.results[0]["out"]
    return np.ascontiguousarray(got.reshape(D, T).T).reshape(1, T, D)
```

```python
from contextlib import ExitStack
import math

import numpy as np

import concourse.bass as bass
from concourse import mybir

ALU = mybir.AluOpType
ACT = mybir.ActivationFunctionType
F32 = mybir.dt.float32
F32R = mybir.dt.float32r
I32 = mybir.dt.int32
AX_X = mybir.AxisListType.X

P = 128
T = 512
D = 1024
KC = D // P
FF = 2816
FC = FF // P
M = 256
TT = T // P
MT = M // P
HD = 64
RING = 4
LEAD = 3
WT = KC * P
DOWN_CUTS = (0, 6, 12, 17, 22)
UP_JOBS = 2 * FC
DOWN_JOBS = 4 * KC
ADA = 512
ADA_STEPS = 2 * 6 * D // ADA
ADA_PER_FFN = 8
CONV_A = 31
CONV_B = 3
PAD_A = CONV_A - 1
PAD_B = CONV_B - 1
TOPK = 128
ROUNDS = TOPK // 8
EPS = 1e-6
SCALE = HD ** -0.5
MASKED = -1e30
TAKEN = -3e38
NO_SINK = -3e38
WI_SCALE = 8 ** -0.5 * HD ** -0.5
TWO_PI = 2 * math.pi
PI_A = 6.28125
PI_B = float(np.float32(np.round((TWO_PI - PI_A) * 2 ** 21) / 2 ** 21))
PI_C = float(np.float32(TWO_PI - PI_A - PI_B))
ROUNDER = 1.5 * 2 ** 23
PI_CLAMP = 3.1415925

COLS = {}
_at = 0
for _name, _n in (("g_ffn1", KC), ("g_mix", KC), ("g_ffn2", KC), ("n1_0", KC), ("n2_0", KC), ("n1_1", KC),
                  ("n2_1", KC), ("g_mem", KC), ("g_q", 1), ("g_k", 1), ("g_mq", 1), ("g_mk", 1), ("g_q2", 1),
                  ("g_k2", 1), ("ln_g", 1), ("ln_b", 1), ("b_dw", 2), ("cln_g", 2), ("cln_b", 2), ("w_dw", 2 * CONV_A),
                  ("sinks", 8), ("conv_w", KC * CONV_B), ("c", KC), ("ada_b", 2 * 6 * KC), ("freq_a", 1), ("freq_b", 1)):
    COLS[_name] = (_at, _n)
    _at += _n
NCOLS = _at
MATS = {"ident": (0, P), "heads": (P, P), "pair_a": (2 * P, P), "pair_b": (3 * P, P), "mask": (4 * P, 2 * P)}
NMATS = 6 * P


class Marks:

    def __init__(self, sem, keys):
        self.sem, self.keys, self.given = sem, list(keys), 0
        self.value = {k: n + 1 for n, k in enumerate(self.keys)}
        assert len(self.value) == len(self.keys)

    def at(self, key):
        assert self.keys[self.given] == key, (key, self.keys[self.given])
        self.given += 1
        return self.sem


def build(nc, A, out):
    ctx = ExitStack()
    with ctx:
        def sem(name):
            return ctx.enter_context(nc.semaphore(name))

        def keep(name, cols, dt=F32):
            return ctx.enter_context(nc.sbuf_tensor(name, [P, cols], dt))

        x = keep("x", KC * T)
        h_hi = keep("h_hi", KC * T, F32R)
        h_lo = keep("h_lo", KC * T, F32R)
        w_raw = keep("w_raw", RING * WT)
        w_hi = keep("w_hi", RING * WT, F32R)
        w_lo = keep("w_lo", RING * WT, F32R)
        tmp = keep("tmp", 4 * T)
        ssum = keep("ssum", T)
        ada_raw = keep("ada_raw", 2 * 2 * ADA)
        ada_sum = keep("ada_sum", ADA)
        ones = keep("ones", P)
        cols = keep("cols", NCOLS)
        modc = keep("modc", 2 * 6 * KC)
        c_act = keep("c_act", KC)
        geff = keep("geff", 4 * KC)
        flat = keep("flat", 3 * KC)
        tiny = keep("tiny", 2)
        identity = keep("identity", P)
        token_std = keep("token_std", TT)
        token_rstd = keep("token_rstd", TT)
        sink8 = keep("sink8", 8)
        small = keep("small", 4 * 4)
        top8 = keep("top8", 8)
        qstd = keep("qstd", 8 * 8)
        qinv = keep("qinv", 8 * 8)
        wi = keep("wi", TT * 8)
        ps = ctx.enter_context(nc.psum_tensor("ps", [P, 8 * T], F32))

        def stage_memory(wanted):
            with ExitStack() as s:
                return [s.enter_context(nc.sbuf_tensor(n, [P, c], dt)) for n, c, dt in wanted]

        hid_hi, hid_lo = stage_memory([("hid_hi", FC * T, F32R), ("hid_lo", FC * T, F32R)])
        (matsA, memx, mh_hi, mh_lo, qA, kA, vA, mq, mk, mv, cosA, sinA, glu, conv, sig, smA, pA, pTA, qnA, hsA, hrA,
         ropA, zeroA) = stage_memory([
            ("matsA", NMATS, F32), ("memx", KC * M, F32), ("mh_hi", KC * M, F32R), ("mh_lo", KC * M, F32R),
            ("qA", 4 * T, F32), ("kA", T, F32), ("vA", TT * P, F32), ("mq", 2 * T, F32), ("mk", 2 * M, F32),
            ("mv", 2 * MT * P, F32), ("cosA", T, F32), ("sinA", T, F32), ("glu", 2 * (PAD_A + T), F32),
            ("conv", 2 * T, F32), ("sig", T, F32), ("smA", 2 * (M + 8), F32), ("pA", 4 * (M + 8), F32),
            ("pTA", 2 * M, F32), ("qnA", 2 * T, F32), ("hsA", 2 * T, F32), ("hrA", T, F32), ("ropA", 2 * T, F32),
            ("zeroA", M, F32)])
        (matsB, qB, kB, vB, qi, ki, cosB, sinB, dmask, score, relu, smB, pB, pTB, qnB, hsB, hrB, ropB, kraw) = \
            stage_memory([
                ("matsB", NMATS, F32), ("qB", 8 * T, F32), ("kB", 2 * T, F32), ("vB", TT * 2 * P, F32),
                ("qi", 4 * T, F32), ("ki", T, F32), ("cosB", T, F32), ("sinB", T, F32), ("dmask", 9 * P, F32),
                ("score", 9 * P, F32), ("relu", 2 * T, F32), ("smB", 2 * T, F32), ("pB", 4 * T, F32),
                ("pTB", 2 * T, F32), ("qnB", 2 * T, F32), ("hsB", 2 * T, F32), ("hrB", T, F32), ("ropB", 2 * T, F32),
                ("kraw", T, F32)])
        zc, c_sb, tap, y_hi, y_lo = stage_memory([
            ("zc", 2 * (PAD_B + T), F32), ("c_sb", 2 * T, F32), ("tap", 2 * T, F32), ("y_hi", KC * T, F32R),
            ("y_lo", KC * T, F32R)])

        SCORE_BANKS = (0, 1, 6)

        def bank(n):
            return ps[:, n * T:(n + 1) * T]

        def chunk(t, k, width=T):
            return t[:, k * width:(k + 1) * width]

        def col(name, n=0, count=1):
            at = COLS[name][0] + n
            return cols[:, at:at + count]

        def f32(ap):
            return ap.bitcast(F32)

        UNITS_A = [("win", j, b, half) for j in range(4) for b in range(TT) for half in range(2)]
        UNITS_A += [("mem", j, b, half) for j in range(2) for b in range(TT) for half in range(2)]
        UNITS_B = [("dsa", j, b, half) for b in range(TT) for j in range(8) for half in range(2)]
        TILES_A = ["g0", "a0", "g1", "a1", "vA", "kA", "qA0", "qA1", "qA2", "qA3", "mq0", "mq1",
                   "mk0", "mk1", "mv0", "mv1"]
        TILES_B = ["ki", "wi", "qi0", "qi1", "qi2", "qi3", "vB0", "vB1", "kB0", "kB1"] + [f"qB{t}" for t in range(8)]
        first_job, at = {}, 0
        for stage, count in (("ffn0", UP_JOBS + DOWN_JOBS), ("mixA", len(TILES_A)), ("outA", KC),
                             ("ffn1", UP_JOBS + DOWN_JOBS), ("mixB", len(TILES_B)), ("outB", KC),
                             ("ffn2", UP_JOBS + DOWN_JOBS), ("mixC", 3 * KC), ("outC", KC),
                             ("ffn3", UP_JOBS + DOWN_JOBS)):
            first_job[stage] = at
            at += count
        JOBS = at
        WEIGHTS = {"outA": "w_out", "outB": "w_out_b", "outC": "w_out_c", "mixA": "w_mix", "mixB": "w_mix_b",
                   "mixC": "w_mix_c"}

        consts_in = sem("consts_in")
        x_in = [sem(f"x_in{k}") for k in range(KC)]
        stage_in = sem("stage_in")
        w_in = [sem(f"w_in{s}") for s in range(RING)]
        w_hi_done = sem("w_hi_done")
        w_lo_done = sem("w_lo_done")
        job_done = sem("job_done")
        silu_done = sem("silu_done")
        hid_done = sem("hid_done")
        hid_hi_done = sem("hid_hi_done")
        hid_lo_done = sem("hid_lo_done")
        x_done = sem("x_done")
        sq_done = sem("sq_done")
        ss_done = sem("ss_done")
        total_done = sem("total_done")
        std_done = sem("std_done")
        rstd_done = sem("rstd_done")
        spread_done = sem("spread_done")
        identity_in = sem("identity_in")
        normed = sem("normed")
        h_hi_done = sem("h_hi_done")
        h_lo_done = sem("h_lo_done")
        ada_in = [sem(f"ada_in{s}") for s in range(2)]
        ada_sum_done = sem("ada_sum_done")
        ada_mm_done = sem("ada_mm_done")
        ada_done = sem("ada_done")
        c_done = sem("c_done")
        z_done = sem("z_done")
        tap_done = sem("tap_done")
        y_done = sem("y_done")
        y_hi_done = sem("y_hi_done")
        y_lo_done = sem("y_lo_done")
        out_done = sem("out_done")
        prep = sem("prep")

        def has_norm(t):
            return t[:2] in ("kA", "qA", "mq", "mk", "kB", "qB", "ki")

        def has_rope(t):
            return t[:2] in ("kA", "qA", "kB", "qB", "ki", "qi")

        def is_token_major(t):
            return t[:2] in ("vA", "mv", "vB", "wi")

        def is_query(t):
            return t[:2] in ("qA", "mq", "qB")

        HEADS = [t for t in TILES_A + TILES_B if has_norm(t) or has_rope(t)]
        NORMS = [t for t in HEADS if has_norm(t) and not is_query(t)]
        SQUARES = [t for t in HEADS if has_norm(t)]
        SCALED = [t for t in HEADS if is_query(t) or t[:2] == "qi"]
        ROPES = [t for t in HEADS if has_rope(t)]
        def in_step_order(tiles, late):
            keyed = []
            for t in tiles:
                lists = TILES_A if t in TILES_A else TILES_B
                keyed.append((lists is TILES_B, lists.index(t) + (late if t == "ki" else 0), t))
            return [t for _, _, t in sorted(keyed, key=lambda k: k[:2])]

        h_sq = Marks(sem("h_sq"), in_step_order(SQUARES, 1.5))
        sq_read = Marks(sem("sq_read"), in_step_order(SQUARES, 1.5))
        h_scaled = Marks(sem("h_scaled"), SCALED)
        h_std = Marks(sem("h_std"), in_step_order(NORMS, 1.5))
        h_rstd = Marks(sem("h_rstd"), in_step_order(NORMS, 1.5))
        h_normed = Marks(sem("h_normed"), in_step_order(NORMS, 1.5))
        h_rot = Marks(sem("h_rot"), in_step_order(ROPES, 1.5))
        h_sin = Marks(sem("h_sin"), in_step_order(ROPES, 1.5))
        h_roped = Marks(sem("h_roped"), in_step_order(ROPES, 1.5))
        evac = Marks(sem("evac"), [t for t in TILES_A + TILES_B if is_token_major(t) or t == "ki" or t[0] == "g"])
        TURNED = [t for t in TILES_A + TILES_B if is_token_major(t)]
        v_turned = Marks(sem("v_turned"), TURNED)
        v_done = Marks(sem("v_done"), TURNED)

        def features_of(t):
            if t == "vA":
                return sig[:, :]
            if t[:2] == "mv":
                return sig[:, int(t[2]) * M:(int(t[2]) + 1) * M]
            return relu[0:8, 0:T] if t == "wi" else chunk(relu, int(t[2]))

        glu_done = Marks(sem("glu_done"), ["a0", "a1"])

        QUERIES = [t for t in TILES_A if is_query(t)], [t for t in TILES_B if is_query(t)]
        UNITS = UNITS_A + UNITS_B

        def weighed_by_act(unit):
            return (unit[0] == "dsa" and unit[2] < 3) or unit[0] == "win"

        u_score = Marks(sem("u_score"), UNITS)
        u_masked = Marks(sem("u_masked"), UNITS)
        u_negmax = Marks(sem("u_negmax"), UNITS)
        u_exp = Marks(sem("u_exp"), UNITS)
        u_inv = Marks(sem("u_inv"), UNITS)
        u_prob_act = Marks(sem("u_prob_act"), [u for u in UNITS if weighed_by_act(u)])
        u_prob_dve = Marks(sem("u_prob_dve"), [u for u in UNITS if not weighed_by_act(u)])
        u_turned = Marks(sem("u_turned"), UNITS)
        u_pt = Marks(sem("u_pt"), UNITS)
        u_out = Marks(sem("u_out"), UNITS)
        GROUPS = [("win", j) for j in range(4)] + [("mem", j) for j in range(2)] + [("dsa", g) for g in range(2 * TT)]

        def group_of(unit):
            kind, j, b, _ = unit
            return (("dsa", 2 * b + j // 4), j % 4) if kind == "dsa" else ((kind, j), b)

        def fills_group(unit):
            return group_of(unit)[1] == 3 and unit[3] == 1

        def group_places(h, group, dest):
            kind, g = group
            bk = bank(4 + GROUPS.index(group) % 2)
            if kind != "dsa":
                return chunk(h, dest), bk
            b, first = g // 2, (g % 2) * 4
            return (h[:, first * T:(first + 4) * T].rearrange("p (k t) -> p k t", k=4)[:, :, b * P:(b + 1) * P],
                    bk.rearrange("p (k t) -> p k t", k=4))
        g_hi = Marks(sem("g_hi"), GROUPS[:4] + ["c0", "c1"] + GROUPS[4:])
        g_lo = Marks(sem("g_lo"), GROUPS[:4] + ["c0", "c1"] + GROUPS[4:])
        IDX = [(b, h) for b in range(1, TT) for h in range(8)]
        i_score = Marks(sem("i_score"), IDX)
        i_relu = Marks(sem("i_relu"), IDX)
        i_sum = Marks(sem("i_sum"), IDX)
        TOPS = []
        for b in range(1, TT):
            TOPS += [(b, "tri")] + [(b, r, s) for r in range(ROUNDS) for s in ("max", "take")] + [(b, "mask")]
        top = Marks(sem("top"), TOPS)
        ROUND_LIST = [(b, r) for b in range(1, TT) for r in range(ROUNDS)]
        TOP_EARLY = 8

        def index_step(m):
            return IDX[(m - 8) * 24 // 10:(m - 7) * 24 // 10] if 8 <= m < 18 else []

        TAB = ["ang", "turns", "whole", "r1", "r2", "r3", "clamp"]
        d_conv = Marks(sem("d_conv"), [(t, c) for t in range(CONV_A) for c in range(2)])
        d_misc = Marks(sem("d_misc"),
                       [("tabA", s) for s in ["pos"] + TAB] + ["mem_sum", "mem_rstd"] +
                       [("mem", k) for k in range(KC)] + ["mem_lo"] +
                       ["qinvA", "ctr0", "ctr1", "conv_rstd0", "conv_rstd1", "conv_n0", "conv_n1", "geff0", "geff1"] +
                       [("tabB", s) for s in ["pos"] + TAB] + ["ki_ctr", "ki_g", "qinvB", "geff2", "geff3"])
        a_misc = Marks(sem("a_misc"),
                       ["sink8", ("tabA", "sin"), ("tabA", "abs"), ("tabA", "cos"), "mem_sq", "mem_std", "mem_hi", "stdA",
                        "conv_sq0", "conv_sq1", "conv_std", "conv_y0", "conv_y1",
                        ("tabB", "sin"), ("tabB", "abs"), ("tabB", "cos"), "stdB"])
        p_misc = Marks(sem("p_misc"), ["mem_total", "conv_total", "conv_var", "ki_total"])

        def turned_of(t, qn):
            return chunk(qn, (h_rot.value[t] - 1) % 2)

        def after(eng, marks, key):
            eng.wait_ge(marks.sem, marks.value[key])

        def after_nth(eng, marks, n):
            if n >= 0:
                eng.wait_ge(marks.sem, n + 1)

        block = ctx.enter_context(nc.Block())


        @block.sync
        def _(sp):
            def load(first, i, step, src):
                slot, width = first % RING, src.shape[-1]
                sp.wait_ge(w_lo_done, i * step + (first + 1))
                sp.dma_start(w_raw[:, slot * WT:slot * WT + width], src).then_inc(w_in[slot], 16)

            def tile_of(w, n):
                return A[w][bass.ds(n, 1), :, :].rearrange("a p n -> (a p) n")

            def ffn(n):
                J = first_job[f"ffn{n}"]

                with sp.Fori(0, FC // 2) as i:
                    for s in range(4):
                        load(J + s, i, 4, tile_of(f"{('gate', 'up')[s % 2]}{n}", i * 2 + s // 2))
                with sp.Fori(0, KC) as j:
                    for s in range(4):
                        load(J + UP_JOBS + s, j, 4,
                             A[f"down{n}"][bass.ds(j, 1), :, DOWN_CUTS[s] * P:DOWN_CUTS[s + 1] * P]
                             .rearrange("a p n -> (a p) n"))

            def project(stage, count):
                J = first_job[stage]
                with sp.Fori(0, count // 4) as i:
                    for s in range(4):
                        load(J + s, i, 4, tile_of(WEIGHTS[stage], i * 4 + s))

            sp.dma_start(cols[:, :], A["cols"]).then_inc(consts_in, 16)
            sp.dma_start(identity[:, :], A["mats"][:, 0:P]).then_inc(identity_in, 16)
            for k in range(KC):
                sp.dma_start(chunk(x, k), A["x"][k]).then_inc(x_in[k], 16)
            ffn(0)
            project("mixA", len(TILES_A))
            project("outA", KC)
            ffn(1)
            J = first_job["mixB"]
            for t, name in enumerate(TILES_B):
                width = KC * 8 if name == "wi" else WT
                load(J + t, 0, 4, A["w_mix_b"][t, :, 0:width])
            project("outB", KC)
            ffn(2)
            project("mixC", 3 * KC)
            project("outC", KC)
            ffn(3)
            for j in range(KC):
                sp.wait_ge(x_done, 8 * 7 + j + 1)
                sp.dma_start(out[j], chunk(x, j)).then_inc(out_done, 16)
            sp.wait_ge(out_done, 16 * KC)

        @block.gpsimd
        def _(pool):
            def ada_load(n, piece):
                pool.wait_ge(ada_sum_done, n * 8 + (2 * piece + 2))
                src = A["ada_w"][bass.ds(n, 1), :, piece * 2 * ADA:(piece + 1) * 2 * ADA]
                pool.dma_start(ada_raw[:, (piece % 2) * 2 * ADA:(piece % 2 + 1) * 2 * ADA],
                             src.rearrange("a p n -> (a p) n")).then_inc(ada_in[piece % 2], 16)

            def ada_steps(n):
                with pool.Fori(n * ADA_PER_FFN, (n + 1) * ADA_PER_FFN) as a:
                    for piece in range(4):
                        ada_load(a, piece)

            ada_steps(0)
            pool.wait_ge(x_done, 16)
            pool.dma_start(memx[:, :], A["mem"]).then_inc(stage_in, 16)
            pool.dma_start(matsA[:, :], A["mats"]).then_inc(stage_in, 16)
            pool.dma_start(ropA[:, 0:T].bitcast(I32), A["positions"]).then_inc(stage_in, 16)
            ada_steps(1)
            pool.wait_ge(x_done, 32)
            pool.dma_start(matsB[:, :], A["mats"]).then_inc(stage_in, 16)
            pool.dma_start(ropB[:, 0:T].bitcast(I32), A["positions_2"]).then_inc(stage_in, 16)
            ada_steps(2)

        @block.tensor
        def _(pe):
            def product(ready, dest, pairs, first, last):
                for n, ((s_hi, s_lo), (m_hi, m_lo)) in enumerate(pairs):
                    if ready:
                        ready(n)
                    pe.matmul(dest, s_hi, m_hi, start=first and n == 0, stop=False)
                    pe.matmul(dest, s_hi, m_lo, start=False, stop=False)
                    mm = pe.matmul(dest, s_lo, m_hi, start=False, stop=last and n == len(pairs) - 1)
                return mm

            def weights(first, k, width=P):
                at = (first % RING) * WT + k * width
                return w_hi[:, at:at + width], w_lo[:, at:at + width]

            def take(first, i=0, step=4):
                pe.wait_ge(w_lo_done, i * step + (first + 1 + RING))

            def moving(k, lo=0, width=T):
                return h_hi[:, k * T + lo:k * T + lo + width], h_lo[:, k * T + lo:k * T + lo + width]

            def norm_total(n):
                pe.wait_ge(ss_done, 9 * (n + 1))
                for b in range(TT):
                    mm = pe.matmul(bank(6)[:, b:b + 1], ssum[:, b * P:(b + 1) * P], ones[:, 0:1], start=True, stop=True)
                mm.then_inc(total_done, 1)
                pe.wait_ge(rstd_done, 2 * (n + 1))
                pe.matmul(bank(6), ones[:, :], chunk(tmp, 3), start=True, stop=True).then_inc(spread_done, 1)

            def ffn(n):
                norm_total({0: 0, 1: 2, 2: 4, 3: 6}[n])
                J = first_job[f"ffn{n}"]
                N = {0: 0, 1: 2, 2: 4, 3: 6}[n]

                def up(i, modulation):
                    for s in range(4):
                        if s % 2 == 0:
                            pe.wait_ge(hid_done, i * 2 + (n * FC + s // 2 + 1))
                        take(J + s, i)
                        ready = (lambda k: pe.wait_ge(h_lo_done, N * KC + k + 1)) if s == 0 else None
                        product(ready, bank(s), [(weights(J + s, k), moving(k)) for k in range(KC)], True, True)\
                            .then_inc(job_done, 1)
                    if modulation:
                        a = i + n * ADA_PER_FFN
                        pe.wait_ge(ada_sum_done, a * 8 + 12)
                        pe.wait_ge(ada_done, a + 1)
                        for q in range(ADA // P):
                            mm = pe.matmul(bank(7)[:, q:q + 1], ada_sum[:, q * P:(q + 1) * P], ones[:, 0:1],
                                           start=True, stop=True)
                        mm.then_inc(ada_mm_done, 1)

                def down(i):
                    for s in range(8):
                        tile, part = s // 4, s % 4
                        js = J + UP_JOBS + s
                        pe.wait_ge(hid_lo_done, n * FC + DOWN_CUTS[part + 1] + 2)
                        if part == 0:
                            pe.wait_ge(x_done, i * 2 + (8 * (2 * n + 1) + tile - 1))
                        take(js, i, 8)
                        c0, c1 = DOWN_CUTS[part], DOWN_CUTS[part + 1]
                        product(None, bank(4 + tile),
                                [(weights(js, c - c0), (chunk(hid_hi, c), chunk(hid_lo, c))) for c in range(c0, c1)],
                                part == 0, part == 3).then_inc(job_done, 1)

                if n < 3:
                    with pe.Fori(0, ADA_PER_FFN) as i:
                        up(i, True)
                with pe.Fori(ADA_PER_FFN if n < 3 else 0, FC // 2) as i:
                    up(i, False)
                with pe.Fori(0, KC // 2) as i:
                    down(i)

            def project(stage, r, ready_sem, ready, hi=h_hi, lo=h_lo):
                J = first_job[stage]
                with pe.Fori(0, KC // 4) as i:
                    for s in range(4):
                        if s == 0:
                            pe.wait_ge(ready_sem, ready)
                        pe.wait_ge(x_done, i * 4 + (8 * r + s - 3))
                        take(J + s, i)
                        product(None, bank(s), [(weights(J + s, k), (chunk(hi, k), chunk(lo, k))) for k in range(KC)],
                                True, True)\
                            .then_inc(job_done, 1)

            def freed(tiles, m):
                if m < 4:
                    return
                t = tiles[m - 4]
                if is_token_major(t):
                    after(pe, v_done, t)
                elif t == "ki" or t[0] == "g":
                    after(pe, evac, t)
                elif t[0] == "a":
                    after(pe, glu_done, t)
                elif is_query(t) or t[:2] == "qi":
                    after(pe, h_scaled, t)
                else:
                    after(pe, h_normed, t)

            def tile_job(tiles, stage, m, n_norm):
                t, js = tiles[m], first_job[stage] + m
                freed(tiles, m)
                take(js)
                ready = (lambda k: pe.wait_ge(h_lo_done, n_norm * KC + k + 1)) if m == 0 else None
                dest = bank(m % 4)
                if t[:2] in ("mk", "mv"):
                    after(pe, d_misc, "mem_lo")
                    mm = product(None, dest[:, 0:M], [(weights(js, k), (chunk(mh_hi, k, M), chunk(mh_lo, k, M)))
                                                      for k in range(KC)], True, True)
                elif t == "wi":
                    mm = product(None, dest[0:8, :], [(weights(js, k, 8), moving(k)) for k in range(KC)], True, True)
                else:
                    mm = product(ready, dest, [(weights(js, k), moving(k)) for k in range(KC)], True, True)
                mm.then_inc(job_done, 1)

            def turn_tile(tiles, m):
                t = tiles[m]
                after(pe, evac, t)
                source = features_of(t)
                rows, blocks = (8 if t == "wi" else P), (MT if t[:2] == "mv" else TT)
                for q in range(blocks):
                    mm = pe.transpose(bank(m % 4)[:, q * rows:(q + 1) * rows], source[:, q * P:(q + 1) * P],
                                      identity[0:rows, 0:rows])
                mm.then_inc(v_turned.at(t), 1)

            def head_sum(t, mats):
                after(pe, h_sq, t)
                n = h_sq.value[t] - 1
                hs = hsA if mats is matsA else hsB
                if is_query(t):
                    if t == "qB0":
                        after(pe, h_std, "kB1")
                    q = QUERIES[t[1] == "B"].index(t)
                    for b in range(TT):
                        at = q * 2 * TT + b * 2
                        mm = pe.matmul(bank(4 if t[1] == "B" else 7)[:, at:at + 2],
                                       hs[:, (n % 2) * T + b * P:(n % 2) * T + (b + 1) * P], mats[:, P:2 * P:HD],
                                       start=True, stop=True)
                    mm.then_inc(sq_read.at(t), 1)
                    return
                after_nth(pe, h_std, h_std.value[t] - 2)
                W = M if t[:2] == "mk" else T
                pe.matmul(bank(4)[:, 0:W], mats[:, P:2 * P], hs[:, (n % 2) * T:(n % 2) * T + W],
                          start=True, stop=True).then_inc(sq_read.at(t), 1)

            def head_turn(t, mats, which, qn):
                after(pe, h_scaled if t in h_scaled.value else h_normed, t)
                n = h_rot.value[t] - 1
                after_nth(pe, h_sin, n - 1)
                at = MATS[which][0]
                pe.matmul(bank(5), mats[:, at:at + P], chunk(qn, n % 2), start=True, stop=True)\
                    .then_inc(h_rot.at(t), 1)

            def attention(units, sc, tr, pv):
                for u in range(len(units) + 4):
                    if u < len(units):
                        sc(units[u])
                    if 3 <= u < len(units) + 3:
                        tr(units[u - 3])
                    if u >= 4:
                        pv(units[u - 4])
                    if units is UNITS_A and u == 27:
                        conv_sums("conv_total", conv)
                    if units is UNITS_A and u == 34:
                        after(pe, a_misc, "conv_sq1")
                        conv_sums("conv_var", hsA)

            def unit_score(unit, q, k, n):
                U = UNITS.index(unit)
                after_nth(pe, u_masked, U - 3)
                pe.matmul(bank(SCORE_BANKS[U % 3])[:, 0:n], q, k, start=True, stop=True).then_inc(u_score.at(unit), 1)

            def unit_turn(unit, p, width, mats, n):
                U = UNITS.index(unit)
                after(pe, u_prob_act if weighed_by_act(unit) else u_prob_dve, unit)
                after_nth(pe, u_pt, U - 2)
                for c in range(n // P):
                    mm = pe.transpose(bank(2 + U % 2)[:, c * P:(c + 1) * P],
                                      p[:, (U % 4) * width + c * P:(U % 4) * width + (c + 1) * P], mats[:, 0:P])
                mm.then_inc(u_turned.at(unit), 1)

            def unit_values(unit, pT, width, vs):
                half = unit[3]
                U = UNITS.index(unit)
                after(pe, u_pt, unit)
                group, at = group_of(unit)
                G = GROUPS.index(group)
                if at == 0 and half == 0 and G >= 2:
                    after(pe, g_lo, GROUPS[G - 2])
                dest = bank(4 + G % 2)[half * HD:(half + 1) * HD, at * P:(at + 1) * P]
                for c, v in enumerate(vs):
                    mm = pe.matmul(dest, v, pT[:, (U % 2) * width + c * P:(U % 2) * width + (c + 1) * P],
                                   start=c == 0, stop=c == len(vs) - 1)
                mm.then_inc(u_out.at(unit), 1)

            pe.wait_ge(prep, 1)
            ffn(0)

            norm_total(1)
            pe.wait_ge(stage_in, 48)
            for m in range(len(TILES_A) + 2):
                if m < len(TILES_A):
                    tile_job(TILES_A, "mixA", m, 1)
                if 1 <= m <= len(TILES_A) and is_token_major(TILES_A[m - 1]):
                    turn_tile(TILES_A, m - 1)
                if m >= 1 and m - 1 < len(TILES_A) and has_norm(TILES_A[m - 1]):
                    head_sum(TILES_A[m - 1], matsA)
                if m >= 2 and has_rope(TILES_A[m - 2]):
                    head_turn(TILES_A[m - 2], matsA, "pair_a", qnA)
                if m == 4:
                    after(pe, d_misc, "mem_sum")
                    pe.matmul(bank(6)[:, 0:M], ones[:, :], ssum[:, 0:M], start=True, stop=True)\
                        .then_inc(p_misc.at("mem_total"), 1)

            def conv_sums(what, src):
                after(pe, d_conv, (CONV_A - 1, 1))
                after(pe, a_misc, "stdA")
                for c in range(2):
                    mm = pe.matmul(bank(7), ones[:, :], chunk(src, c), start=c == 0, stop=c == 1)
                mm.then_inc(p_misc.at(what), 1)

            def scoreA(unit):
                kind, j, b, half = unit
                rows = slice(half * HD, (half + 1) * HD)
                if kind == "win":
                    n, lo = (P, 0) if b == 0 else (2 * P, (b - 1) * P)
                    unit_score(unit, qA[rows, j * T + b * P:j * T + (b + 1) * P], kA[rows, lo:lo + n], n)
                else:
                    unit_score(unit, mq[rows, j * T + b * P:j * T + (b + 1) * P], mk[rows, j * M:(j + 1) * M], M)

            def turnA(unit):
                unit_turn(unit, pA, M + 8, matsA, P if unit[0] == "win" and unit[2] == 0 else 2 * P)

            def valuesA(unit):
                kind, j, b, half = unit
                if kind == "win":
                    tiles = [b] if b == 0 else [b - 1, b]
                    vs = [vA[:, q * P + half * HD:q * P + (half + 1) * HD] for q in tiles]
                else:
                    vs = [mv[:, (j * MT + q) * P + half * HD:(j * MT + q) * P + (half + 1) * HD] for q in range(MT)]
                unit_values(unit, pTA, M, vs)

            after(pe, h_roped, "qA3")
            after(pe, h_normed, "mk1")
            after(pe, h_scaled, "mq1")
            after(pe, v_done, "mv1")
            attention(UNITS_A, scoreA, turnA, valuesA)
            project("outA", 2, g_lo.sem, g_lo.value[("mem", 1)])
            ffn(1)

            norm_total(3)
            pe.wait_ge(stage_in, 80)
            for m in range(len(TILES_B) + 2):
                if m < len(TILES_B):
                    tile_job(TILES_B, "mixB", m, 3)
                if 1 <= m <= len(TILES_B) and is_token_major(TILES_B[m - 1]):
                    turn_tile(TILES_B, m - 1)
                if m == 1:
                    after(pe, evac, "ki")
                    pe.matmul(bank(6), matsB[:, P:2 * P], kraw[:, :], start=True, stop=True)\
                        .then_inc(p_misc.at("ki_total"), 1)
                if m == 2:
                    head_sum("ki", matsB)
                if 2 <= m <= len(TILES_B) and has_norm(TILES_B[m - 1]):
                    head_sum(TILES_B[m - 1], matsB)
                if m == 3:
                    head_turn("ki", matsB, "pair_b", qnB)
                if m >= 3 and has_rope(TILES_B[m - 2]):
                    head_turn(TILES_B[m - 2], matsB, "pair_b", qnB)
                if m == 8:
                    after(pe, h_roped, "qi3")
                for b, h in index_step(m):
                    n = (b + 1) * P
                    I = IDX.index((b, h))
                    after_nth(pe, i_relu, I - 2)
                    rows = slice((h % 2) * HD, (h % 2 + 1) * HD)
                    pe.matmul(bank(6 + I % 2)[:, 0:n], qi[rows, (h // 2) * T + b * P:(h // 2) * T + (b + 1) * P],
                              ki[rows, 0:n], start=True, stop=True).then_inc(i_score.at((b, h)), 1)

            def scoreB(unit):
                _, j, b, half = unit
                rows = slice(half * HD, (half + 1) * HD)
                n = (b + 1) * P
                unit_score(unit, qB[rows, j * T + b * P:j * T + (b + 1) * P],
                           kB[rows, (j // 4) * T:(j // 4) * T + n], n)

            def turnB(unit):
                unit_turn(unit, pB, T, matsB, (unit[2] + 1) * P)

            def valuesB(unit):
                _, j, b, half = unit
                at = (j // 4) * P + half * HD
                unit_values(unit, pTB, T, [vB[:, (j // 4) * TT * P + q * P + half * HD:
                                              (j // 4) * TT * P + q * P + (half + 1) * HD] for q in range(b + 1)])

            after(pe, h_roped, "qB7")
            attention(UNITS_B, scoreB, turnB, valuesB)
            project("outB", 4, g_lo.sem, g_lo.value[GROUPS[-1]])
            ffn(2)

            norm_total(5)
            J = first_job["mixC"]
            role_done = (c_done, z_done, y_done)
            with pe.Fori(0, 2) as i:
                for q in range(12):
                    pe.wait_ge(role_done[(q - 4) % 3], i * 4 + ((q - 4) // 3 + 3))
                    take(J + q, i, 12)
                    ready = (lambda k: pe.wait_ge(h_lo_done, 5 * KC + k + 1)) if q == 0 else None
                    product(ready, bank(q % 4), [(weights(J + q, k), moving(k)) for k in range(KC)], True, True)\
                        .then_inc(job_done, 1)
            project("outC", 6, y_lo_done, KC + 2, y_hi, y_lo)
            ffn(3)

        @block.scalar
        def _(act):
            def split(first, i, step):
                slot = first % RING
                act.wait_ge(w_in[slot], i * (16 * step // RING) + 16 * (first // RING + 1))
                act.wait_ge(job_done, i * step + (first + 1))
                act.activation(chunk(w_hi, slot, WT), chunk(w_raw, slot, WT), ACT.Copy).then_inc(w_hi_done, 1)

            def lead(first, i=0, step=4):
                if first + LEAD < JOBS or step > 4:
                    split(first + LEAD, i, step)

            def square_x(r, j, parity):
                act.wait_ge(x_done, j + (8 * r + 1))
                if not (r == 0 and isinstance(j, int) and j == 0):
                    act.wait_ge(ss_done, j + 9 * r)
                act.activation(chunk(tmp, parity), x[:, bass.ds(j * T, T)], ACT.Square).then_inc(sq_done, 1)

            def norm(n, shift):
                act.wait_ge(total_done, n + 1)
                act.activation(token_std[:, :], bank(6)[:, 0:TT], ACT.Sqrt, bias=tiny[:, 0:1], scale=1.0 / D)\
                    .then_inc(std_done, 1)
                for k in range(KC):
                    act.wait_ge(normed, KC * n + k + 1)
                    act.activation(chunk(h_hi, k), chunk(tmp, k % 3), ACT.Identity, bias=shift[:, k:k + 1])\
                        .then_inc(h_hi_done, 1)

            def ffn(n, shift):
                norm({0: 0, 1: 2, 2: 4, 3: 6}[n], shift)
                J = first_job[f"ffn{n}"]

                def up(i):
                    for s in range(4):
                        lead(J + s, i)
                        u = s // 2
                        F = n * FC + u
                        if s % 2 == 0:
                            act.wait_ge(job_done, i * 4 + (J + s + 1 + RING))
                            act.wait_ge(hid_done, i * 2 + (F + 1))
                            act.activation(chunk(tmp, u), bank(s), ACT.Silu).then_inc(silu_done, 1)
                        else:
                            act.wait_ge(hid_done, i * 2 + (F + 3))
                            act.activation(hid_hi[:, bass.ds(i * (2 * T) + u * T, T)], chunk(tmp, 2 + u), ACT.Copy)\
                                .then_inc(hid_hi_done, 1)

                def down(i, last):
                    for s in range(8):
                        if not (last and s >= 8 - LEAD):
                            split(J + UP_JOBS + s + LEAD, i, 8)
                        if s % 4 == 3 and n < 3:
                            square_x(2 * n + 1, i * 2 + s // 4, s // 4)

                with act.Fori(0, FC // 2) as i:
                    up(i)
                if n < 3:
                    with act.Fori(0, KC // 2) as i:
                        down(i, False)
                else:
                    with act.Fori(0, KC // 2 - 1) as i:
                        down(i, False)
                    down(KC // 2 - 1, True)

            def project(stage, r):
                J = first_job[stage]
                with act.Fori(0, KC // 4) as i:
                    for s in range(4):
                        lead(J + s, i)
                        square_x(r, i * 4 + s, s % 2)

            def tables(which, rop, sin, cos):
                after(act, d_misc, (which, "clamp"))
                act.activation(sin[:, :], rop[:, 0:T], ACT.Sin).then_inc(a_misc.at((which, "sin")), 1)
                act.activation(rop[:, T:2 * T], rop[:, 0:T], ACT.Abs).then_inc(a_misc.at((which, "abs")), 1)
                after(act, a_misc, (which, "abs"))
                act.activation(cos[:, :], rop[:, T:2 * T], ACT.Sin, bias=tiny[:, 1:2], scale=-1.0)\
                    .then_inc(a_misc.at((which, "cos")), 1)

            def head_square(t, js, hs, src=None):
                n = h_sq.value[t] - 1
                if src is None:
                    act.wait_ge(job_done, js + 1 + RING)
                W = M if t[:2] == "mk" else T
                after_nth(act, sq_read, n - 2)
                act.activation(hs[:, (n % 2) * T:(n % 2) * T + W], bank(js % 4)[:, 0:W] if src is None else src,
                               ACT.Square).then_inc(h_sq.at(t), 1)

            def head_scale(t, js, gain, dest):
                if has_norm(t):
                    after(act, h_sq, t)
                else:
                    act.wait_ge(job_done, js + 1 + RING)
                if has_rope(t):
                    after_nth(act, h_sin, h_rot.value[t] - 3)
                    after_nth(act, h_rot, h_rot.value[t] - 3)
                act.activation(dest, bank(js % 4), ACT.Copy, scale=gain).then_inc(h_scaled.at(t), 1)

            def keep_tile(t, m, dest, scale=1.0):
                after(act, v_turned, t)
                act.activation(dest, bank(m % 4)[:, 0:{"mv": M, "wi": TT * 8}.get(t[:2], T)], ACT.Copy, scale=scale)\
                    .then_inc(v_done.at(t), 1)

            def query_std(which, count):
                after(act, sq_read, QUERIES[which == "B"][-1])
                act.activation(qstd[:, 0:count], bank(4 if which == "B" else 7)[:, 0:count], ACT.Sqrt, bias=tiny[:, 0:1],
                               scale=1.0 / HD).then_inc(a_misc.at("std" + which), 1)

            def head_std(t, hr):
                n = h_sq.value[t] - 1
                after(act, sq_read, t)
                if h_std.value[t] > 1:
                    after(act, h_normed, h_std.keys[h_std.value[t] - 2])
                W = M if t[:2] == "mk" else T
                act.activation(hr[:, 0:W], bank(4)[:, 0:W], ACT.Sqrt, bias=tiny[:, 0:1], scale=1.0 / HD)\
                    .then_inc(h_std.at(t), 1)

            def exp_unit(unit, sm, p, width, n):
                U = UNITS.index(unit)
                after(act, u_negmax, unit)
                after_nth(act, u_turned, U - 4)
                s = U % 4
                act.activation(p[:, (U % 4) * width:(U % 4) * width + n], sm[:, (U % 2) * width:(U % 2) * width + n],
                               ACT.Exp, bias=small[:, 4 + s:5 + s], scale=SCALE, accum_out=small[:, 8 + s:9 + s])\
                    .then_inc(u_exp.at(unit), 1)

            def weigh_unit(unit, p, width, n):
                U = UNITS.index(unit)
                s, at = U % 4, (U % 4) * width
                after(act, u_inv, unit)
                act.activation(p[:, at:at + n], p[:, at:at + n], ACT.Copy, scale=small[:, 12 + s:13 + s])\
                    .then_inc(u_prob_act.at(unit), 1)

            def keep_turned(unit, pT, width, n):
                U = UNITS.index(unit)
                after(act, u_turned, unit)
                after_nth(act, u_out, U - 2)
                act.activation(pT[:, (U % 2) * width:(U % 2) * width + n], bank(2 + U % 2)[:, 0:n], ACT.Copy)\
                    .then_inc(u_pt.at(unit), 1)

            def group_high(unit, dest):
                group = group_of(unit)[0]
                after(act, u_out, unit)
                to, bk = group_places(h_hi, group, dest)
                act.activation(to, bk, ACT.Copy).then_inc(g_hi.at(group), 1)

            def attention(units, sm, p, width, pT, pT_width, size, dest):
                for u in range(len(units) + 5):
                    if 3 <= u < len(units) + 3:
                        keep_turned(units[u - 3], pT, pT_width, size(units[u - 3]))
                    if 1 <= u < len(units) + 1 and weighed_by_act(units[u - 1]):
                        weigh_unit(units[u - 1], p, width, size(units[u - 1]))
                    if u < len(units):
                        kind, j, b, half = units[u]
                        exp_unit(units[u], sm, p, width, size(units[u]) + (1 if kind == "win" else 0))
                    if u >= 5 and fills_group(units[u - 5]):
                        group_high(units[u - 5], dest(*units[u - 5][:2]))
                    if units is UNITS_A:
                        conv_part(u)

            act.wait_ge(consts_in, 16)
            act.activation(c_act[:, :], col("c", 0, KC), ACT.Silu).then_inc(prep, 1)
            act.activation(sink8[:, :], col("sinks", 0, 8), ACT.Copy, scale=1.0 / SCALE).then_inc(a_misc.at("sink8"), 1)
            for j in range(KC):
                act.wait_ge(x_in[j], 16)
                square_x(0, j, j % 2)
            for j in range(LEAD):
                act.wait_ge(w_in[j], 16)
                act.activation(chunk(w_hi, j, WT), chunk(w_raw, j, WT), ACT.Copy).then_inc(w_hi_done, 1)
            none = flat[:, 0:KC]
            ffn(0, none)

            norm(1, none)
            act.wait_ge(stage_in, 48)
            tables("tabA", ropA, sinA, cosA)
            act.activation(qA[:, :], memx[:, :], ACT.Square).then_inc(a_misc.at("mem_sq"), 1)
            J = first_job["mixA"]
            for m in range(len(TILES_A) + 2):
                if m < len(TILES_A):
                    t = TILES_A[m]
                    lead(J + m)
                    if has_norm(t):
                        head_square(t, J + m, hsA)
                    if t[:2] in ("vA", "mv"):
                        act.wait_ge(job_done, J + m + 1 + RING)
                        if t == "vA":
                            after(act, glu_done, "a1")
                        else:
                            after(act, v_turned, "vA")
                        act.activation(features_of(t), bank(m % 4)[:, 0:T if t == "vA" else M], ACT.Copy)\
                            .then_inc(evac.at(t), 1)
                    elif t[0] == "g":
                        act.wait_ge(job_done, J + m + 1 + RING)
                        if t == "g1":
                            after(act, glu_done, "a0")
                        act.activation(sig[:, :], bank(m % 4), ACT.Sigmoid).then_inc(evac.at(t), 1)
                if 1 <= m and m - 1 < len(TILES_A) and TILES_A[m - 1] in h_std.value:
                    head_std(TILES_A[m - 1], hrA)
                if m < len(TILES_A) and is_query(TILES_A[m]):
                    t = TILES_A[m]
                    head_scale(t, J + m, col("g_q" if t[0] == "q" else "g_mq"),
                               turned_of(t, qnA) if t[0] == "q" else chunk(mq, int(t[2])))
                if 1 <= m <= len(TILES_A) and is_token_major(TILES_A[m - 1]):
                    t = TILES_A[m - 1]
                    keep_tile(t, m - 1, vA[:, :] if t == "vA" else chunk(mv, int(t[2]), M))
                if m == 13:
                    query_std("A", 8 * len(QUERIES[0]))
                if m == 5:
                    after(act, p_misc, "mem_total")
                    act.activation(ssum[:, M:2 * M], bank(6)[:, 0:M], ACT.Sqrt, bias=tiny[:, 0:1], scale=1.0 / D)\
                        .then_inc(a_misc.at("mem_std"), 1)
                if m == 7:
                    after(act, d_misc, ("mem", KC - 1))
                    act.activation(mh_hi[:, :], memx[:, :], ACT.Copy).then_inc(a_misc.at("mem_hi"), 1)

            def conv_part(u):
                if u in (30, 31):
                    c = u - 30
                    after(act, d_misc, f"ctr{c}")
                    act.activation(chunk(hsA, c), chunk(conv, c), ACT.Square).then_inc(a_misc.at(f"conv_sq{c}"), 1)
                if u == 35:
                    after(act, p_misc, "conv_var")
                    act.activation(hrA[:, :], bank(7), ACT.Sqrt, bias=tiny[:, 0:1], scale=1.0 / (2 * P))\
                        .then_inc(a_misc.at("conv_std"), 1)
                if u == 42:
                    for c in range(2):
                        after(act, d_misc, f"conv_n{c}")
                        act.activation(chunk(conv, c), chunk(conv, c), ACT.Silu, bias=col("cln_b", c))\
                            .then_inc(a_misc.at(f"conv_y{c}"), 1)
                if u == 43:
                    for c in range(2):
                        after(act, a_misc, f"conv_y{c}")
                        act.activation(chunk(h_hi, 4 + c), chunk(conv, c), ACT.Copy).then_inc(g_hi.at(f"c{c}"), 1)

            act.wait_ge(job_done, J + len(TILES_A) + RING)
            attention(UNITS_A, smA, pA, M + 8, pTA, M,
                      lambda u: P if u[0] == "win" and u[2] == 0 else 2 * P,
                      lambda kind, j: j if kind == "win" else 6 + j)
            project("outA", 2)
            ffn(1, none)

            norm(3, modc[:, 0:KC])
            act.wait_ge(stage_in, 80)
            tables("tabB", ropB, sinB, cosB)
            J = first_job["mixB"]
            for m in range(len(TILES_B) + 2):
                if m < len(TILES_B):
                    t = TILES_B[m]
                    lead(J + m)
                    if t == "ki":
                        act.wait_ge(job_done, J + m + 1 + RING)
                        act.activation(kraw[:, :], bank(m % 4), ACT.Copy).then_inc(evac.at(t), 1)
                    elif t == "wi":
                        act.wait_ge(job_done, J + m + 1 + RING)
                        act.activation(features_of(t), bank(m % 4)[0:8, :], ACT.Copy).then_inc(evac.at(t), 1)
                    elif t[:2] == "vB":
                        act.wait_ge(job_done, J + m + 1 + RING)
                        if t == "vB0":
                            after(act, v_turned, "wi")
                        act.activation(features_of(t), bank(m % 4), ACT.Copy).then_inc(evac.at(t), 1)
                    elif has_norm(t):
                        head_square(t, J + m, hsB)
                if m == 1:
                    after(act, d_misc, "ki_ctr")
                    head_square("ki", J, hsB, src=kraw[:, :])
                if m == 2:
                    head_std("ki", hrB)
                if 2 <= m <= len(TILES_B) and TILES_B[m - 1] in h_std.value:
                    head_std(TILES_B[m - 1], hrB)
                if 1 <= m <= len(TILES_B) and is_token_major(TILES_B[m - 1]):
                    t = TILES_B[m - 1]
                    if t == "wi":
                        keep_tile(t, m - 1, wi[:, :], WI_SCALE)
                    else:
                        keep_tile(t, m - 1, chunk(vB, int(t[2])))
                if m < len(TILES_B) and TILES_B[m][:2] in ("qB", "qi"):
                    t = TILES_B[m]
                    head_scale(t, J + m, col("g_q2") if t[:2] == "qB" else 1.0, turned_of(t, qnB))
                for b, h in index_step(m):
                    n = (b + 1) * P
                    I = IDX.index((b, h))
                    after(act, i_score, (b, h))
                    after_nth(act, i_sum, I - 2)
                    act.activation(relu[:, (I % 2) * T:(I % 2) * T + n], bank(6 + I % 2)[:, 0:n], ACT.Relu)\
                        .then_inc(i_relu.at((b, h)), 1)
            query_std("B", 8 * len(QUERIES[1]))
            attention(UNITS_B, smB, pB, T, pTB, T, lambda u: (u[2] + 1) * P, lambda kind, j: j)
            project("outB", 4)
            ffn(2, modc[:, 3 * KC:4 * KC])

            norm(5, modc[:, 6 * KC:7 * KC])
            J = first_job["mixC"]
            with act.Fori(0, 2) as i:
                for q in range(12):
                    lead(J + q, i, 12)
                    l, role = q // 3, q % 3
                    if role == 0:
                        act.wait_ge(job_done, i * 12 + (J + q + 1 + RING))
                        act.wait_ge(z_done, i * 4 + (l + 1))
                        act.activation(chunk(c_sb, l % 2), bank(q % 4), ACT.Copy).then_inc(c_done, 1)
                    if role == 2:
                        act.wait_ge(y_done, i * 4 + (l + 3))
                        act.activation(y_hi[:, bass.ds(i * (4 * T) + l * T, T)], chunk(tap, l % 2), ACT.Copy).then_inc(y_hi_done, 1)
            project("outC", 6)
            ffn(3, modc[:, 9 * KC:10 * KC])

        @block.vector
        def _(dve):
            def split(first, i=0, step=4):
                slot = first % RING
                dve.wait_ge(w_hi_done, i * step + (first + 1))
                dve.tensor_tensor(chunk(w_lo, slot, WT), chunk(w_raw, slot, WT), f32(chunk(w_hi, slot, WT)),
                                  ALU.subtract).then_inc(w_lo_done, 1)

            def lead(first, i=0, step=4):
                if first + LEAD < JOBS or step > 4:
                    split(first + LEAD, i, step)

            def sum_x(r, j, parity):
                dve.wait_ge(sq_done, j + (8 * r + 1))
                dve.wait_ge(ss_done, j + (9 * r + 1))
                dve.tensor_tensor(ssum[:, :], ssum[:, :], chunk(tmp, parity), ALU.add).then_inc(ss_done, 1)

            def clear_sum(r):
                if r:
                    dve.wait_ge(total_done, r)
                dve.memset(ssum[:, :], 0.0).then_inc(ss_done, 1)

            def update_x(r, j, b, gates, job, i, step):
                dve.wait_ge(job_done, i * step + (job + 1 + RING))
                here = x[:, bass.ds(j * T, T)]
                dve.scalar_tensor_tensor(here, bank(b), gates[:, bass.ds(j, 1)], here, ALU.mult, ALU.add)\
                    .then_inc(x_done, 1)

            def norm(n, gain, shift):
                dve.wait_ge(std_done, n + 1)
                dve.reciprocal(token_rstd[:, :], token_std[:, :]).then_inc(rstd_done, 1)
                dve.wait_ge(rstd_done, 2 * n + 1)
                dve.tensor_tensor(chunk(tmp, 3).rearrange("p (b t) -> p b t", b=TT),
                                  identity[:, :].unsqueeze(1).to_broadcast([P, TT, P]),
                                  token_rstd[:, :].unsqueeze(2).to_broadcast([P, TT, P]), ALU.mult)\
                    .then_inc(rstd_done, 1)
                dve.wait_ge(spread_done, n + 1)
                rstd = bank(6)
                for k in range(KC + 1):
                    if k < KC:
                        if k > 2:
                            dve.wait_ge(h_lo_done, KC * n + k - 2)
                        dve.scalar_tensor_tensor(chunk(tmp, k % 3), chunk(x, k), gain[:, k:k + 1], rstd,
                                                 ALU.mult, ALU.mult).then_inc(normed, 1)
                    if k:
                        dve.wait_ge(h_hi_done, KC * n + k)
                        dve.scalar_tensor_tensor(chunk(h_lo, k - 1), chunk(tmp, (k - 1) % 3), shift[:, k - 1:k],
                                                 f32(chunk(h_hi, k - 1)), ALU.add, ALU.subtract)\
                            .then_inc(h_lo_done, 1)

            def ffn(n, gain, shift, gates):
                norm({0: 0, 1: 2, 2: 4, 3: 6}[n], gain, shift)
                J = first_job[f"ffn{n}"]

                def modulate(a, k):
                    piece = k // 2
                    w = ada_raw[:, (piece % 2) * 2 * ADA + (k % 2) * ADA:(piece % 2) * 2 * ADA + (k % 2 + 1) * ADA]
                    dve.wait_ge(ada_in[piece % 2], a * 32 + 16 * (piece // 2 + 1))
                    if k == 0:
                        dve.wait_ge(ada_mm_done, a + 1)
                        dve.tensor_scalar(ada_sum[:, :], w, c_act[:, 0:1], None, ALU.mult).then_inc(ada_sum_done, 1)
                    else:
                        dve.wait_ge(ada_sum_done, a * 8 + (k + 4))
                        dve.scalar_tensor_tensor(ada_sum[:, :], w, c_act[:, k:k + 1], ada_sum[:, :],
                                                 ALU.mult, ALU.add).then_inc(ada_sum_done, 1)

                def hidden_low(i, u):
                    dve.wait_ge(hid_hi_done, i * 2 + (n * FC + u + 1))
                    at = bass.ds(i * (2 * T) + u * T, T)
                    dve.tensor_tensor(hid_lo[:, at], chunk(tmp, 2 + u), f32(hid_hi[:, at]), ALU.subtract)\
                        .then_inc(hid_lo_done, 1)

                def up(i, modulation):
                    for s in range(4):
                        lead(J + s, i)
                        u = s // 2
                        if modulation:
                            for k in range(2 * s, 2 * s + 2):
                                modulate(i + n * ADA_PER_FFN, k)
                        if s % 2:
                            dve.wait_ge(job_done, i * 4 + (J + s + 1 + RING))
                            dve.wait_ge(silu_done, i * 2 + (n * FC + u + 1))
                            dve.wait_ge(hid_lo_done, i * 2 + (n * FC + u + 1))
                            dve.tensor_tensor(chunk(tmp, 2 + u), chunk(tmp, u), bank(s), ALU.mult)\
                                .then_inc(hid_done, 1)
                            hidden_low(i, u)
                    if modulation:
                        a = i + n * ADA_PER_FFN
                        dve.wait_ge(ada_mm_done, a + 2)
                        dve.tensor_tensor(modc[:, bass.ds(a * 4, 4)], bank(7)[:, 0:4],
                                          cols[:, bass.ds(a * 4 + COLS["ada_b"][0], 4)], ALU.add)\
                            .then_inc(ada_done, 1)

                def down(i, last):
                    for s in range(8):
                        if not (last and s >= 8 - LEAD):
                            split(J + UP_JOBS + s + LEAD, i, 8)
                        if s % 4 == 3:
                            t = s // 4
                            update_x(2 * n + 1, i * 2 + t, 4 + t, gates, J + UP_JOBS + s, i, 8)
                            if n < 3:
                                sum_x(2 * n + 1, i * 2 + t, t)

                if n < 3:
                    with dve.Fori(0, ADA_PER_FFN) as i:
                        up(i, True)
                with dve.Fori(ADA_PER_FFN if n < 3 else 0, FC // 2) as i:
                    up(i, False)
                if n < 3:
                    clear_sum(2 * n + 1)
                    with dve.Fori(0, KC // 2) as i:
                        down(i, False)
                else:
                    with dve.Fori(0, KC // 2 - 1) as i:
                        down(i, False)
                    down(KC // 2 - 1, True)

            def project(stage, r, gates):
                J = first_job[stage]
                clear_sum(r)
                with dve.Fori(0, KC // 4) as i:
                    for s in range(4):
                        lead(J + s, i)
                        update_x(r, i * 4 + s, s, gates, J + s, i, 4)
                        sum_x(r, i * 4 + s, s % 2)

            def tables(which, rop, freq):
                one, two = chunk(rop, 0), chunk(rop, 1)

                def did(step):
                    return d_misc.at((which, step))

                def stands(step):
                    after(dve, d_misc, (which, step))

                dve.tensor_copy(two, one.bitcast(I32)).then_inc(did("pos"), 1)
                stands("pos")
                dve.tensor_scalar(one, two, freq, None, ALU.mult).then_inc(did("ang"), 1)
                stands("ang")
                dve.tensor_scalar(two, one, 1.0 / TWO_PI, ROUNDER, ALU.mult, ALU.add).then_inc(did("turns"), 1)
                stands("turns")
                dve.tensor_scalar(two, two, ROUNDER, None, ALU.subtract).then_inc(did("whole"), 1)
                for part, step, before in ((PI_A, "r1", "whole"), (PI_B, "r2", "r1"), (PI_C, "r3", "r2")):
                    stands(before)
                    dve.scalar_tensor_tensor(one, two, -part, one, ALU.mult, ALU.add).then_inc(did(step), 1)
                stands("r3")
                dve.tensor_scalar(one, one, PI_CLAMP, -PI_CLAMP, ALU.min, ALU.max).then_inc(did("clamp"), 1)

            def head_norm(t, js, gain, hr, dest, src=None, bias=None):
                W = M if t[:2] == "mk" else T
                after(dve, h_std, t)
                dve.reciprocal(hr[:, 0:W], hr[:, 0:W]).then_inc(h_rstd.at(t), 1)
                after(dve, h_rstd, t)
                if has_rope(t):
                    after_nth(dve, h_sin, h_rot.value[t] - 3)
                if bias is None:
                    dve.scalar_tensor_tensor(dest, bank(js % 4)[:, 0:W], gain, hr[:, 0:W], ALU.mult, ALU.mult)\
                        .then_inc(h_normed.at(t), 1)
                else:
                    dve.scalar_tensor_tensor(dest, src, gain, hr[:, 0:W], ALU.mult, ALU.mult)\
                        .then_inc(d_misc.at("ki_g"), 1)
                    after(dve, d_misc, "ki_g")
                    dve.tensor_scalar(dest, dest, bias, None, ALU.add).then_inc(h_normed.at(t), 1)

            def head_rope(t, qn, rop, sin, cos, dest):
                n = h_rot.value[t] - 1
                after(dve, h_scaled if t in h_scaled.value else h_normed, t)
                after_nth(dve, h_roped, n - 1)
                dve.tensor_tensor(chunk(rop, 0), chunk(qn, n % 2), cos[:, :], ALU.mult)
                after(dve, h_rot, t)
                dve.tensor_tensor(chunk(rop, 1), bank(5), sin[:, :], ALU.mult).then_inc(h_sin.at(t), 1)
                after(dve, h_sin, t)
                dve.tensor_tensor(dest, chunk(rop, 0), chunk(rop, 1), ALU.add).then_inc(h_roped.at(t), 1)

            def query_inverse(which, count):
                after(dve, a_misc, "std" + which)
                dve.reciprocal(qinv[:, 0:count], qstd[:, 0:count]).then_inc(d_misc.at("qinv" + which), 1)
                after(dve, d_misc, "qinv" + which)

            def mask_unit(unit, sm, width, mask, n, sink, tile):
                U = UNITS.index(unit)
                s, at = U % 4, (U % 2) * width
                after(dve, u_score, unit)
                after_nth(dve, u_exp, U - 2)
                if sink is not None:
                    dve.tensor_copy(sm[:, at + n:at + n + 1], sink)
                q = tile * 2 * TT + unit[2] * 2 + unit[3]
                dve.tensor_tensor_reduce(sm[:, at:at + n], bank(SCORE_BANKS[U % 3])[:, 0:n], mask, qinv[:, q:q + 1],
                                         NO_SINK, ALU.add, ALU.max,
                                         small[:, s:s + 1]).then_inc(u_masked.at(unit), 1)
                after(dve, u_masked, unit)
                if sink is not None:
                    dve.tensor_scalar(small[:, 4 + s:5 + s], small[:, s:s + 1], sink, -SCALE, ALU.max, ALU.mult)\
                        .then_inc(u_negmax.at(unit), 1)
                else:
                    dve.tensor_scalar(small[:, 4 + s:5 + s], small[:, s:s + 1], -SCALE, None, ALU.mult)\
                        .then_inc(u_negmax.at(unit), 1)

            def weigh_unit(unit, p, width, n):
                U = UNITS.index(unit)
                s, at = U % 4, (U % 4) * width
                after(dve, u_exp, unit)
                dve.reciprocal(small[:, 12 + s:13 + s], small[:, 8 + s:9 + s]).then_inc(u_inv.at(unit), 1)
                if not weighed_by_act(unit):
                    after(dve, u_inv, unit)
                    dve.tensor_scalar(p[:, at:at + n], p[:, at:at + n], small[:, 12 + s:13 + s], None, ALU.mult)\
                        .then_inc(u_prob_dve.at(unit), 1)

            def group_low(unit, dest):
                group = group_of(unit)[0]
                after(dve, g_hi, group)
                to, bk = group_places(h_lo, group, dest)
                high, _ = group_places(h_hi, group, dest)
                dve.tensor_tensor(to, bk, f32(high), ALU.subtract).then_inc(g_lo.at(group), 1)

            def attention(units, mask, weigh, dest):
                for u in range(len(units) + 6):
                    if u < len(units):
                        mask(units[u])
                    if 1 <= u < len(units) + 1:
                        weigh(units[u - 1])
                    if units is UNITS_A:
                        conv_part(u)
                    elif TOP_EARLY + u < len(ROUND_LIST):
                        take_top(*ROUND_LIST[TOP_EARLY + u])
                    if u >= 6 and fills_group(units[u - 6]):
                        group_low(units[u - 6], dest(*units[u - 6][:2]))

            dve.memset(ones[:, :], 1.0).then_inc(job_done, RING)
            dve.memset(tiny[:, 0:1], EPS).then_inc(w_lo_done, RING)
            dve.memset(tiny[:, 1:2], math.pi / 2).then_inc(hid_done, 2)
            dve.memset(top8[:, 5:6], 0.0).then_inc(hid_lo_done, 2)
            dve.memset(top8[:, 6:7], 0.0).then_inc(tap_done, 4)
            dve.memset(top8[:, 7:8], 0.0).then_inc(y_lo_done, 2)
            dve.memset(flat[:, 0:KC], 0.0).then_inc(ada_sum_done, 4)
            dve.memset(flat[:, KC:2 * KC], 0.5).then_inc(ada_mm_done, 1)
            dve.memset(flat[:, 2 * KC:3 * KC], 1.0).then_inc(ada_done, 1)
            dve.memset(top8[:, 0:1], 0.0).then_inc(x_done, KC)
            dve.memset(top8[:, 1:2], 0.0).then_inc(c_done, 2)
            dve.memset(top8[:, 2:3], 0.0).then_inc(z_done, 2)
            dve.memset(top8[:, 3:4], 0.0).then_inc(y_done, 2)
            none, half, whole = (flat[:, n * KC:(n + 1) * KC] for n in range(3))
            clear_sum(0)
            for j in range(KC):
                sum_x(0, j, j % 2)
            for j in range(LEAD):
                split(j)
            dve.wait_ge(prep, 1)
            dve.wait_ge(identity_in, 16)
            ffn(0, col("g_ffn1", 0, KC), none, half)

            norm(1, col("g_mix", 0, KC), none)
            dve.wait_ge(stage_in, 48)
            tables("tabA", ropA, col("freq_a"))
            dve.memset(glu[:, 0:PAD_A], 0.0)
            dve.memset(glu[:, PAD_A + T:2 * PAD_A + T], 0.0)
            dve.memset(zeroA[:, :], 0.0)
            after(dve, a_misc, ("tabA", "cos"))
            J = first_job["mixA"]
            GAINS = {"kA": "g_k", "mk": "g_mk"}
            taps = [(t, c) for t in range(CONV_A) for c in range(2)]

            def conv_tap(t, c):
                src = glu[:, c * (PAD_A + T) + t:c * (PAD_A + T) + t + T]
                w = col("w_dw", c * CONV_A + t)
                if t == 0:
                    dve.tensor_scalar(chunk(conv, c), src, w, col("b_dw", c), ALU.mult, ALU.add)\
                        .then_inc(d_conv.at((t, c)), 1)
                else:
                    after(dve, d_conv, (t - 1, c))
                    dve.scalar_tensor_tensor(chunk(conv, c), src, w, chunk(conv, c), ALU.mult, ALU.add)\
                        .then_inc(d_conv.at((t, c)), 1)

            for m in range(len(TILES_A) + 2):
                if m < len(TILES_A):
                    t = TILES_A[m]
                    lead(J + m)
                    if t[0] == "a":
                        c = int(t[1])
                        after(dve, evac, f"g{c}")
                        dve.wait_ge(job_done, J + m + 1 + RING)
                        dve.tensor_tensor(glu[:, c * (PAD_A + T) + PAD_A:(c + 1) * (PAD_A + T)], sig[:, :], bank(m % 4),
                                          ALU.mult).then_inc(glu_done.at(t), 1)
                if m >= 1 and m - 1 < len(TILES_A) and TILES_A[m - 1] in h_normed.value:
                    t = TILES_A[m - 1]
                    dest = chunk(mk, int(t[2]), M) if t[:2] == "mk" else turned_of(t, qnA)
                    head_norm(t, J + m - 1, col(GAINS[t[:2]]), hrA, dest)
                if m >= 2 and has_rope(TILES_A[m - 2]):
                    t = TILES_A[m - 2]
                    head_rope(t, qnA, ropA, sinA, cosA, kA[:, :] if t == "kA" else chunk(qA, int(t[2])))
                if m == 1:
                    after(dve, a_misc, "mem_sq")
                    dve.tensor_reduce(ssum[:, 0:M], qA[:, :].rearrange("p (k t) -> p t k", k=KC), AX_X, ALU.add)\
                        .then_inc(d_misc.at("mem_sum"), 1)
                if m == 6:
                    after(dve, a_misc, "mem_std")
                    dve.reciprocal(ssum[:, M:2 * M], ssum[:, M:2 * M]).then_inc(d_misc.at("mem_rstd"), 1)
                    after(dve, d_misc, "mem_rstd")
                    for k in range(KC):
                        dve.scalar_tensor_tensor(chunk(memx, k, M), chunk(memx, k, M), col("g_mem", k), ssum[:, M:2 * M],
                                                 ALU.mult, ALU.mult).then_inc(d_misc.at(("mem", k)), 1)
                if m == 8:
                    after(dve, a_misc, "mem_hi")
                    dve.tensor_tensor(mh_lo[:, :], memx[:, :], f32(mh_hi[:, :]), ALU.subtract)\
                        .then_inc(d_misc.at("mem_lo"), 1)
                if m == 4:
                    after(dve, glu_done, "a1")
                if m == len(TILES_A) - 1:
                    query_inverse("A", 8 * len(QUERIES[0]))
                if 4 <= m < 14:
                    for t, c in taps[(m - 4) * 3:(m - 3) * 3]:
                        conv_tap(t, c)

            def conv_part(u):
                for t, c in taps[30 + u * 32 // 26:30 + (u + 1) * 32 // 26]:
                    conv_tap(t, c)
                if u in (28, 29):
                    c = u - 28
                    after(dve, p_misc, "conv_total")
                    dve.scalar_tensor_tensor(chunk(conv, c), bank(7), -1.0 / (2 * P), chunk(conv, c), ALU.mult,
                                             ALU.add).then_inc(d_misc.at(f"ctr{c}"), 1)
                if u in (37, 38):
                    part = hrA[:, (u - 37) * T // 2:(u - 36) * T // 2]
                    after(dve, a_misc, "conv_std")
                    dve.reciprocal(part, part).then_inc(d_misc.at(f"conv_rstd{u - 37}"), 1)
                if u in (39, 40):
                    c = u - 39
                    after(dve, d_misc, "conv_rstd1")
                    dve.scalar_tensor_tensor(chunk(conv, c), chunk(conv, c), col("cln_g", c), hrA[:, :], ALU.mult,
                                             ALU.mult).then_inc(d_misc.at(f"conv_n{c}"), 1)
                if u == 44:
                    for c in range(2):
                        after(dve, g_hi, f"c{c}")
                        dve.tensor_tensor(chunk(h_lo, 4 + c), chunk(conv, c), f32(chunk(h_hi, 4 + c)), ALU.subtract)\
                            .then_inc(g_lo.at(f"c{c}"), 1)

            def maskA(unit):
                kind, j, b, half_ = unit
                if kind == "win":
                    lo, n = (P, P) if b == 0 else (0, 2 * P)
                    at = MATS["mask"][0] + lo
                    mask_unit(unit, smA, M + 8, matsA[:, at:at + n], n, sink8[:, j + 4 * half_:j + 4 * half_ + 1], j)
                else:
                    mask_unit(unit, smA, M + 8, zeroA[:, :], M, None, 4 + j)

            after(dve, a_misc, "sink8")
            attention(UNITS_A, maskA,
                      lambda u: weigh_unit(u, pA, M + 8, P if u[0] == "win" and u[2] == 0 else 2 * P),
                      lambda kind, j: j if kind == "win" else 6 + j)
            project("outA", 2, whole)
            ffn(1, col("g_ffn2", 0, KC), none, half)

            def gains(n, g, scale_at, need):
                dve.wait_ge(ada_done, need + 1)
                dve.scalar_tensor_tensor(geff[:, n * KC:(n + 1) * KC], modc[:, scale_at * KC:(scale_at + 1) * KC], 1.0,
                                         col(g, 0, KC), ALU.add, ALU.mult).then_inc(d_misc.at(f"geff{n}"), 1)

            gains(0, "n1_0", 1, 12)
            gains(1, "n2_0", 4, 12)
            after(dve, d_misc, "geff1")
            norm(3, geff[:, 0:KC], modc[:, 0:KC])
            dve.wait_ge(stage_in, 80)
            tables("tabB", ropB, col("freq_b"))
            after(dve, a_misc, ("tabB", "cos"))
            J = first_job["mixB"]
            starts = {1: 0, 2: 2 * P, 3: 5 * P}

            def index_sum(b, h):
                n = (b + 1) * P
                I = IDX.index((b, h))
                s = score[:, starts[b]:starts[b] + n]
                r = relu[:, (I % 2) * T:(I % 2) * T + n]
                w = wi[:, b * 8 + h:b * 8 + h + 1]
                after(dve, i_relu, (b, h))
                if h == 0:
                    dve.tensor_scalar(s, r, w, None, ALU.mult).then_inc(i_sum.at((b, h)), 1)
                else:
                    after(dve, i_sum, (b, h - 1))
                    dve.scalar_tensor_tensor(s, r, w, s, ALU.mult, ALU.add).then_inc(i_sum.at((b, h)), 1)

            def take_top(b, r):
                n = (b + 1) * P
                s = score[:, starts[b]:starts[b] + n]
                if r == 0:
                    after(dve, i_sum, (b, 7))
                    at = MATS["mask"][0] + P
                    dve.tensor_tensor(s[:, n - P:n], s[:, n - P:n], matsB[:, at:at + P], ALU.add)\
                        .then_inc(top.at((b, "tri")), 1)
                after(dve, top, (b, "tri") if r == 0 else (b, r - 1, "take"))
                dve.max(top8[:, :], s).then_inc(top.at((b, r, "max")), 1)
                after(dve, top, (b, r, "max"))
                dve.match_replace(s, top8[:, :], s, TAKEN).then_inc(top.at((b, r, "take")), 1)
                if r == ROUNDS - 1:
                    after(dve, top, (b, r, "take"))
                    dve.tensor_scalar(dmask[:, starts[b]:starts[b] + n], s, TAKEN / 2, MASKED, ALU.is_gt, ALU.mult)\
                        .then_inc(top.at((b, "mask")), 1)

            for m in range(len(TILES_B) + 2):
                if m < len(TILES_B):
                    lead(J + m)
                if m == 1:
                    after(dve, p_misc, "ki_total")
                    dve.scalar_tensor_tensor(kraw[:, :], bank(6), -1.0 / HD, kraw[:, :], ALU.mult, ALU.add)\
                        .then_inc(d_misc.at("ki_ctr"), 1)
                if m == 2:
                    head_norm("ki", J, col("ln_g"), hrB, turned_of("ki", qnB), src=kraw[:, :], bias=col("ln_b"))
                if 2 <= m <= len(TILES_B):
                    t = TILES_B[m - 1]
                    if t in h_normed.value:
                        head_norm(t, J + m - 1, col("g_k2"), hrB, turned_of(t, qnB))
                if m == 3:
                    head_rope("ki", qnB, ropB, sinB, cosB, ki[:, :])
                if m >= 3 and has_rope(TILES_B[m - 2]):
                    t = TILES_B[m - 2]
                    whole_of = {"kB": kB, "qB": qB, "qi": qi}[t[:2]]
                    head_rope(t, qnB, ropB, sinB, cosB, chunk(whole_of, int(t[2])))
                for b, h in index_step(m):
                    index_sum(b, h)
                if 12 <= m < 12 + TOP_EARLY // 2:
                    for b, r in ROUND_LIST[2 * (m - 12):2 * (m - 11)]:
                        take_top(b, r)

            def maskB(unit):
                _, j, b, half_ = unit
                if b == 0:
                    at = MATS["mask"][0] + P
                    mask_unit(unit, smB, T, matsB[:, at:at + P], P, None, j)
                else:
                    if j == 0 and half_ == 0:
                        after(dve, top, (b, "mask"))
                    n = (b + 1) * P
                    mask_unit(unit, smB, T, dmask[:, starts[b]:starts[b] + n], n, None, j)

            query_inverse("B", 8 * len(QUERIES[1]))
            attention(UNITS_B, maskB, lambda u: weigh_unit(u, pB, T, (u[2] + 1) * P), lambda kind, j: j)
            project("outB", 4, modc[:, 2 * KC:3 * KC])
            ffn(2, geff[:, KC:2 * KC], modc[:, 3 * KC:4 * KC], modc[:, 5 * KC:6 * KC])

            gains(2, "n1_1", 7, 24)
            gains(3, "n2_1", 10, 24)
            after(dve, d_misc, "geff3")
            norm(5, geff[:, 2 * KC:3 * KC], modc[:, 6 * KC:7 * KC])
            for l in range(2):
                dve.memset(zc[:, l * (PAD_B + T):l * (PAD_B + T) + PAD_B], 0.0)
            J = first_job["mixC"]
            with dve.Fori(0, 2) as i:
                for q in range(12):
                    lead(J + q, i, 12)
                    l, role = q // 3, q % 3
                    z0 = (l % 2) * (PAD_B + T)
                    y = chunk(tap, l % 2)
                    if role == 1:
                        dve.wait_ge(c_done, i * 4 + (l + 3))
                        dve.wait_ge(job_done, i * 12 + (J + q + 1 + RING))
                        dve.wait_ge(tap_done, i * 12 + (3 * l + 1))
                        dve.tensor_tensor(zc[:, z0 + PAD_B:z0 + PAD_B + T], chunk(c_sb, l % 2), bank(q % 4), ALU.mult)\
                            .then_inc(z_done, 1)
                        dve.wait_ge(z_done, i * 4 + (l + 3))
                        for t in range(CONV_B):
                            w = cols[:, bass.ds(i * (4 * CONV_B) + (COLS["conv_w"][0] + l * CONV_B + t), 1)]
                            z = zc[:, z0 + t:z0 + t + T]
                            if t == 0:
                                dve.wait_ge(y_lo_done, i * 4 + (l + 1))
                                dve.tensor_scalar(y, z, w, None, ALU.mult).then_inc(tap_done, 1)
                            else:
                                dve.wait_ge(tap_done, i * 12 + (3 * l + t + 4))
                                dve.scalar_tensor_tensor(y, z, w, y, ALU.mult, ALU.add).then_inc(tap_done, 1)
                    if role == 2:
                        dve.wait_ge(job_done, i * 12 + (J + q + 1 + RING))
                        dve.wait_ge(tap_done, i * 12 + (3 * l + 7))
                        dve.tensor_tensor(y, y, bank(q % 4), ALU.mult).then_inc(y_done, 1)
                        dve.wait_ge(y_hi_done, i * 4 + (l + 1))
                        at = bass.ds(i * (4 * T) + l * T, T)
                        dve.tensor_tensor(y_lo[:, at], y, f32(y_hi[:, at]), ALU.subtract).then_inc(y_lo_done, 1)
            project("outC", 6, modc[:, 8 * KC:9 * KC])
            ffn(3, geff[:, 3 * KC:4 * KC], modc[:, 9 * KC:10 * KC], modc[:, 11 * KC:12 * KC])


def matrices():
    m = np.zeros((P, NMATS), np.float32)
    m[:, 0:P] = np.eye(P)
    f = np.zeros((P, 2), np.float32)
    for p in range(P):
        head, d = p // HD, p % HD
        m[p, P + head * HD:P + (head + 1) * HD] = 1.0
        for which, width, theta, n in ((2, 16, 500000.0, 0), (3, HD, 10000.0, 1)):
            if d < width:
                h = width // 2
                partner = head * HD + (d + h) % width
                m[partner, which * P + p] = -1.0 if d < h else 1.0
                f[p, n] = theta ** (-(d % h) / h)
    q, k = np.arange(P)[:, None], np.arange(2 * P)[None, :]
    rel = q + P - k
    m[:, 4 * P:] = np.where((rel >= 0) & (rel < P), 0.0, MASKED)
    return m, f


def columns(v):
    v = np.asarray(v).reshape(-1, P)
    return v.T


def tiles(w, cols=P):
    w = np.asarray(w)
    return np.ascontiguousarray(w.reshape(w.shape[0] // P, P, -1, cols).transpose(2, 1, 0, 3)).reshape(
        w.shape[1] // cols, P, -1)


def heads_apart(w, axis, order):
    w = np.moveaxis(np.asarray(w), axis, 0)
    w = w.reshape((-1, HD) + w.shape[1:])[order]
    return np.moveaxis(w.reshape((-1,) + w.shape[2:]), 0, axis)


def layout(v):
    a = {}
    mats, freq = matrices()
    a["mats"] = mats
    g = {k: np.asarray(t) for k, t in v.items()}
    twice = lambda t: np.concatenate([t, t]).reshape(P, 1)
    parts = {
        "g_ffn1": columns(g["g_ffn1"]), "g_mix": columns(g["g_mix"]), "g_ffn2": columns(g["g_ffn2"]),
        "n1_0": columns(g["norm1_g_2"][0]), "n2_0": columns(g["norm2_g_2"][0]), "n1_1": columns(g["norm1_g_2"][1]),
        "n2_1": columns(g["norm2_g_2"][1]), "g_mem": columns(g["g_mem"]), "g_q": twice(g["g_q"][0]),
        "g_k": twice(g["g_k"][0]), "g_mq": twice(g["g_mq"][0]), "g_mk": twice(g["g_mk"][0]),
        "g_q2": twice(g["attn_q_norm_g_2"][0]), "g_k2": twice(g["attn_k_norm_g_2"][0]),
        "ln_g": twice(g["idx_k_ln_g_2"][0]), "ln_b": twice(g["idx_k_ln_b_2"][0]), "b_dw": columns(g["b_dw"]),
        "cln_g": columns(g["g_conv_ln"]), "cln_b": columns(g["b_conv_ln"]),
        "w_dw": g["w_dw"][0].reshape(CONV_A, 2, P).transpose(2, 1, 0).reshape(P, -1),
        "sinks": np.broadcast_to(g["sinks"].reshape(1, 8), (P, 8)),
        "conv_w": g["conv_w_2"][0].reshape(CONV_B, KC, P).transpose(2, 1, 0).reshape(P, -1),
        "c": columns(g["c_2"]), "ada_b": columns(g["ada_b_2"]), "freq_a": freq[:, 0:1], "freq_b": freq[:, 1:2],
    }
    a["cols"] = np.ascontiguousarray(np.concatenate([parts[k] for k in COLS], axis=1))
    a["x"] = np.ascontiguousarray(g["x"][0].T).reshape(KC, P, T)
    a["mem"] = np.ascontiguousarray(g["mem"][0].T.reshape(KC, P, M).transpose(1, 0, 2)).reshape(P, KC * M)
    a["positions"] = np.ascontiguousarray(np.broadcast_to(g["positions"].reshape(1, T), (P, T)))
    a["positions_2"] = np.ascontiguousarray(np.broadcast_to(g["positions_2"].reshape(1, T), (P, T)))
    ffns = [("w_ffn1_gate", "w_ffn1_up", "w_ffn1_down", 0), ("w_ffn2_gate", "w_ffn2_up", "w_ffn2_down", 0),
            ("ffn_w_gate_2", "ffn_w_up_2", "ffn_w_down_2", 0), ("ffn_w_gate_2", "ffn_w_up_2", "ffn_w_down_2", 1)]
    for n, (gate, up, down, l) in enumerate(ffns):
        a[f"gate{n}"], a[f"up{n}"], a[f"down{n}"] = tiles(g[gate][l]), tiles(g[up][l]), tiles(g[down][l])
    w = g["w_in"][0]
    q, k, vv, u, mq = np.split(w, [512, 640, 768, 1280], axis=1)
    order = [h for j in range(4) for h in (j, j + 4)]
    ua, ug = u[:, 0:2 * P], u[:, 2 * P:]
    q = heads_apart(q, 1, order)
    w = np.concatenate([ug[:, :P], ua[:, :P], ug[:, P:], ua[:, P:], vv, k, q, mq, g["w_mem_kv"][0]], axis=1)
    a["w_mix"] = tiles(w)
    w = g["w_out"][0]
    a["w_out"] = tiles(np.concatenate([heads_apart(w[:512], 0, order), w[512:]], axis=0))
    w = g["attn_w_in_2"][0]
    q, k, vv, qi, ki, wi = np.split(w, [1024, 1280, 1536, 2048, 2112], axis=1)
    order = [h for pair in range(2) for r in range(4) for h in (8 * pair + r, 8 * pair + 4 + r)]
    q = heads_apart(q, 1, order)
    main = tiles(np.concatenate([ki, ki, qi, vv, k, q], axis=1))
    wt = np.zeros((1, P, WT), np.float32)
    wt[:, :, :KC * 8] = tiles(wi, 8)
    a["w_mix_b"] = np.concatenate([main[0:1], wt, main[1:]], axis=0)
    a["w_out_b"] = tiles(heads_apart(g["attn_w_out_2"][0], 0, order))
    b_gate, c_gate, uu = (tiles(t) for t in np.split(g["conv_w_in_2"][0], 3, axis=1))
    a["w_mix_c"] = np.ascontiguousarray(np.stack([c_gate, uu, b_gate], axis=1)).reshape(3 * KC, P, WT)
    a["w_out_c"] = tiles(g["conv_w_out_2"][0])
    a["ada_w"] = np.concatenate([tiles(g["ada_w_2"][l], ADA) for l in range(2)], axis=0)
    return a


def kernel(**inputs):
    import concourse.bacc as bacc
    from concourse.bass_utils import run_bass_kernel_spmd

    arrays = layout(inputs)
    nc = bacc.Bacc("TRN2", target_bir_lowering=False, num_devices=1)
    aps = {n: nc.dram_tensor(f"in_{n}", a.shape, mybir.dt.from_np(a.dtype), kind="ExternalInput").ap()
           for n, a in arrays.items()}
    out = nc.dram_tensor("out", (KC, P, T), F32, kind="ExternalOutput").ap()
    build(nc, aps, out)
    result = run_bass_kernel_spmd(nc, [{f"in_{n}": a for n, a in arrays.items()}], core_ids=[0])
    got = result.results[0]["out"]
    return np.ascontiguousarray(got.reshape(D, T).T).reshape(1, T, D)
```
